# Optimizing a Trainium2 kernel written in Bass

```python
import jax, jax.numpy as jnp
from jax import lax
import numpy as np

D_MODEL = 1024
BATCH = 1
SEQ = 1024
DEPTH = 1

MIX_WIDTH = D_MODEL
ATTN_WIDTH = MIX_WIDTH // 2
RET_WIDTH = MIX_WIDTH - ATTN_WIDTH
HEAD_DIM = 64
N_Q_HEADS = ATTN_WIDTH // HEAD_DIM
N_KV_HEADS = 2
GQA_GROUP = N_Q_HEADS // N_KV_HEADS
WINDOW = 128
BLOCK = 128
RET_HEADS = 4
RET_DK = RET_WIDTH // RET_HEADS
RET_DV = RET_WIDTH // RET_HEADS
CHUNK = 128
D_FF = 4 * D_MODEL
EPS = 1e-6
NEG_INF = -1e30
IN_SPLITS = (ATTN_WIDTH, N_KV_HEADS * HEAD_DIM, N_KV_HEADS * HEAD_DIM, RET_HEADS * RET_DK, RET_HEADS * RET_DK, RET_HEADS * RET_DV, RET_WIDTH)
IN_WIDTH = ATTN_WIDTH + 2 * N_KV_HEADS * HEAD_DIM + 2 * RET_HEADS * RET_DK + RET_HEADS * RET_DV + RET_WIDTH

kernel_name = 'hybrid_swa_sink_retention_adaln_block'

def rms_norm(x, gain):
    xf = x.astype(jnp.float32)
    y = xf * lax.rsqrt(jnp.mean(xf * xf, axis=-1, keepdims=True) + EPS)
    return (y * gain.astype(jnp.float32)).astype(x.dtype)

def alibi_slopes(n):
    return jnp.exp2(-8.0 * jnp.arange(1, n + 1, dtype=jnp.float32) / n)

def with_previous_block(t):
    prev = jnp.concatenate([jnp.zeros_like(t[:, :1]), t[:, :-1]], axis=1)
    return jnp.concatenate([prev, t], axis=2)

def sliding_window_sink_attention(q, k, v, q_gain, k_gain, sinks):
    b, s = q.shape[0], q.shape[1]
    nb = s // BLOCK
    q = rms_norm(q, q_gain).reshape(b, nb, BLOCK, N_KV_HEADS, GQA_GROUP, HEAD_DIM)
    k = with_previous_block(rms_norm(k, k_gain).reshape(b, nb, BLOCK, N_KV_HEADS, HEAD_DIM))
    v = with_previous_block(v.reshape(b, nb, BLOCK, N_KV_HEADS, HEAD_DIM))
    scores = jnp.einsum('bnqkgd,bnskd->bnkgqs', q, k, preferred_element_type=jnp.float32) * (HEAD_DIM ** -0.5)
    q_pos = jnp.arange(BLOCK)[:, None]
    k_pos = jnp.arange(2 * BLOCK)[None, :]
    dist = q_pos + BLOCK - k_pos
    valid = (dist >= 0) & (dist < WINDOW)
    valid = valid[None] & ((jnp.arange(nb)[:, None, None] > 0) | (k_pos[None] >= BLOCK))
    bias = -alibi_slopes(N_Q_HEADS)[:, None, None] * dist.astype(jnp.float32)
    scores = scores + bias.reshape(N_KV_HEADS, GQA_GROUP, BLOCK, 2 * BLOCK)
    scores = jnp.where(valid[None, :, None, None], scores, NEG_INF)
    sink = jnp.broadcast_to(sinks.astype(jnp.float32).reshape(N_KV_HEADS, GQA_GROUP, 1, 1), scores.shape[:-1] + (1,))
    probs = jax.nn.softmax(jnp.concatenate([scores, sink], axis=-1), axis=-1)[..., :-1]
    out = jnp.einsum('bnkgqs,bnskd->bnqkgd', probs.astype(v.dtype), v)
    return out.reshape(b, s, ATTN_WIDTH)

def multiscale_retention(q, k, v, g, norm_gain):
    b, s = q.shape[0], q.shape[1]
    nc = s // CHUNK
    f32 = jnp.float32
    qc = q.astype(f32).reshape(b, nc, CHUNK, RET_HEADS, RET_DK)
    kc = k.astype(f32).reshape(b, nc, CHUNK, RET_HEADS, RET_DK) * (RET_DK ** -0.5)
    vc = v.astype(f32).reshape(b, nc, CHUNK, RET_HEADS, RET_DV)
    log_gamma = jnp.log1p(-jnp.exp2(-5.0 - jnp.arange(RET_HEADS, dtype=f32)))
    idx = jnp.arange(CHUNK, dtype=f32)
    rel = idx[:, None] - idx[None, :]
    decay_in = jnp.where(rel >= 0, jnp.exp(log_gamma[:, None, None] * jnp.maximum(rel, 0.0)), 0.0)
    q_decay = jnp.exp(log_gamma[None, :] * (idx[:, None] + 1.0))
    k_decay = jnp.exp(log_gamma[None, :] * (CHUNK - 1.0 - idx[:, None]))
    chunk_decay = jnp.exp(log_gamma * CHUNK)
    inner = jnp.einsum('bnihd,bnjhd->bnhij', qc, kc) * decay_in
    o_inner = jnp.einsum('bnhij,bnjhe->bnihe', inner, vc)
    kv = jnp.einsum('bnjhd,bnjhe->bnhde', kc * k_decay[:, :, None], vc)

    def step(state, kv_n):
        return chunk_decay[None, :, None, None] * state + kv_n, state

    _, prev = lax.scan(step, jnp.zeros((b, RET_HEADS, RET_DK, RET_DV), f32), jnp.moveaxis(kv, 1, 0))
    prev = jnp.moveaxis(prev, 0, 1)
    o_cross = jnp.einsum('bnihd,bnhde->bnihe', qc, prev) * q_decay[:, :, None]
    o = (o_inner + o_cross).reshape(b, s, RET_HEADS, RET_DV)
    mu = jnp.mean(o, axis=-1, keepdims=True)
    var = jnp.mean(jnp.square(o - mu), axis=-1, keepdims=True)
    o = ((o - mu) * lax.rsqrt(var + EPS)).reshape(b, s, RET_WIDTH) * norm_gain.astype(f32)
    return (jax.nn.silu(g.astype(f32)) * o).astype(q.dtype)

def hybrid_layer(x, c_act, norm1_g, norm2_g, w_ada, b_ada, w_in, q_norm_g, k_norm_g, sinks, ret_norm_g, w_out, w_mlp1, w_mlp2):
    b, s = x.shape[0], x.shape[1]
    ada = (c_act @ w_ada + b_ada)[:, None, :]
    shift1, scale1, gate1, shift2, scale2, gate2 = jnp.split(ada, 6, axis=-1)
    h = rms_norm(x, norm1_g) * (1.0 + scale1) + shift1
    proj = h @ w_in
    offsets = np.cumsum(IN_SPLITS)[:-1].tolist()
    aq, ak, av, rq, rk, rv, rg = jnp.split(proj, offsets, axis=-1)
    attn = sliding_window_sink_attention(
        aq.reshape(b, s, N_Q_HEADS, HEAD_DIM),
        ak.reshape(b, s, N_KV_HEADS, HEAD_DIM),
        av.reshape(b, s, N_KV_HEADS, HEAD_DIM),
        q_norm_g, k_norm_g, sinks)
    ret = multiscale_retention(
        rq.reshape(b, s, RET_HEADS, RET_DK),
        rk.reshape(b, s, RET_HEADS, RET_DK),
        rv.reshape(b, s, RET_HEADS, RET_DV),
        rg, ret_norm_g)
    mixed = jnp.concatenate([attn.astype(x.dtype), ret.astype(x.dtype)], axis=-1) @ w_out
    x = x + gate1 * mixed
    h = rms_norm(x, norm2_g) * (1.0 + scale2) + shift2
    x = x + gate2 * (jnp.square(jax.nn.relu(h @ w_mlp1)) @ w_mlp2)
    return x

def setup_inputs(seed: int = 0) -> dict:
    key = jax.random.key(seed)
    ks = jax.random.split(key, 14)
    f32 = jnp.float32

    def normal(k, shape, scale):
        return jax.random.normal(k, shape, f32) * scale

    return {
        'x': normal(ks[0], (BATCH, SEQ, D_MODEL), 1.0),
        'c': normal(ks[1], (BATCH, D_MODEL), 1.0),
        'norm1_g': 1.0 + normal(ks[2], (DEPTH, D_MODEL), 0.05),
        'norm2_g': 1.0 + normal(ks[3], (DEPTH, D_MODEL), 0.05),
        'w_ada': normal(ks[4], (DEPTH, D_MODEL, 6 * D_MODEL), 0.5 * D_MODEL ** -0.5),
        'b_ada': normal(ks[5], (DEPTH, 6 * D_MODEL), 0.02),
        'w_in': normal(ks[6], (DEPTH, D_MODEL, IN_WIDTH), D_MODEL ** -0.5),
        'q_norm_g': 1.0 + normal(ks[7], (DEPTH, HEAD_DIM), 0.05),
        'k_norm_g': 1.0 + normal(ks[8], (DEPTH, HEAD_DIM), 0.05),
        'sinks': normal(ks[9], (DEPTH, N_Q_HEADS), 0.5),
        'ret_norm_g': 1.0 + normal(ks[10], (DEPTH, RET_WIDTH), 0.05),
        'w_out': normal(ks[11], (DEPTH, MIX_WIDTH, D_MODEL), MIX_WIDTH ** -0.5),
        'w_mlp1': normal(ks[12], (DEPTH, D_MODEL, D_FF), D_MODEL ** -0.5),
        'w_mlp2': normal(ks[13], (DEPTH, D_FF, D_MODEL), D_FF ** -0.5),
    }

def reference(x, c, norm1_g, norm2_g, w_ada, b_ada, w_in, q_norm_g, k_norm_g, sinks, ret_norm_g, w_out, w_mlp1, w_mlp2):
    c_act = jax.nn.silu(c)
    for layer in range(DEPTH):
        x = hybrid_layer(x, c_act, norm1_g[layer], norm2_g[layer], w_ada[layer], b_ada[layer], w_in[layer],
                         q_norm_g[layer], k_norm_g[layer], sinks[layer], ret_norm_g[layer], w_out[layer],
                         w_mlp1[layer], w_mlp2[layer])
    return x


_drawn_inputs = setup_inputs


def setup_inputs(seed=0):
    import zlib

    import numpy as np

    out = dict(_drawn_inputs(seed))
    spreads = {}
    factors = {'norm1_g': 3.787,
     'q_norm_g': 8.0,
     'k_norm_g': 8.0,
     'sinks': 200.0,
     'ret_norm_g': 7.364,
     'norm2_g': 8.0}
    for name, (base, spread) in spreads.items():
        noise = np.random.default_rng([zlib.crc32(name.encode()), seed]).standard_normal(out[name].shape)
        drawn = base * np.exp(spread * noise) if base else spread * noise
        out[name] = __import__('jax').numpy.asarray(drawn.astype(out[name].dtype))
    for name, factor in factors.items():
        out[name] = (out[name] * factor).astype(out[name].dtype)
    return out
```

```python
from contextlib import ExitStack

import concourse.bass as bass
from concourse import mybir

F32 = mybir.dt.float32
F32R = mybir.dt.float32r
ALU = mybir.AluOpType
ACT = mybir.ActivationFunctionType
AX_X = mybir.AxisListType.X

P = 128
D = 1024
S = 1024
KT = D // P
NB = S // P
HALF = 512
HEAD = 64
NQ, NKV = 8, 2
GQA = NQ // NKV
RH = 4
FF = 4 * D
EPS = 1e-6
IN_W = 2816
TQ, TK, TV, RQ, RK, RV, RG = 0, 4, 5, 6, 10, 14, 18
N_PROJ = IN_W // P
N_OUT = D // P
QUARTERS = 4
T_OUT = N_PROJ
T_MLP = T_OUT + N_OUT
N_TILES = T_MLP + QUARTERS * 2 * KT
SLOPES = [2.0 ** (-8.0 * (h + 1) / NQ) for h in range(NQ)]
MASKED = 1e33
C_ID, C_ONE, C_BLK, C_DIST, C_DEC, C_QDEC, C_KDEC = 0, 128, 256, 384, 640, 1152, 1664
C_CHUNK = 1668
C_W = 1672
V_BADA, V_N1, V_N2, V_RET, V_C, V_QG, V_KG, V_ROWS = 0, 48, 56, 64, 68, 76, 77, 78


def shape_constants():
    import numpy as np

    c = np.zeros((P, C_W), np.float64)
    i = np.arange(P)
    c[:, C_ID:C_ID + P] = np.eye(P)
    c[:, C_ONE:C_ONE + P] = 1.0
    c[:, C_BLK:C_BLK + P] = (i[:, None] // HEAD) == (i[None, :] // HEAD)
    dist = i[:, None] + P - np.arange(2 * P)[None, :]
    c[:, C_DIST:C_DIST + 2 * P] = np.where((dist >= 0) & (dist < P), dist, MASKED)
    for h in range(RH):
        lg = np.log1p(-(2.0 ** (-5.0 - h)))
        rel = i[None, :] - i[:, None]
        c[:, C_DEC + h * P:C_DEC + (h + 1) * P] = np.where(rel >= 0, np.exp(lg * np.maximum(rel, 0)), 0) * P ** -0.5
        c[:, C_QDEC + h * P:C_QDEC + (h + 1) * P] = np.exp(lg * (i + 1.0))[None, :]
        c[:, C_KDEC + h] = np.exp(lg * (P - 1.0 - i)) * P ** -0.5
        c[:, C_CHUNK + h] = np.exp(lg * P)
    return c.astype(np.float32)


def hybrid_layer(nc, x, c, norm1_g, norm2_g, w_ada, b_ada, w_in, q_norm_g, k_norm_g, sinks,
                 ret_norm_g, w_out, w_mlp1, w_mlp2, consts, x_spill, out):
    ctx = ExitStack()
    with ctx:
        KB = 1024
        BASE = 16512
        ACTS, REG, WTS, TMP = BASE, BASE + 64 * KB, BASE + 160 * KB, BASE + 184 * KB

        def at(name, shape, off, dt=F32):
            return nc.alloc_sbuf_tensor_at(name, [P] + shape, dt, offset=off)

        act_hi = at("act_hi", [KT, S], ACTS, F32R)
        act_lo = at("act_lo", [KT, S], ACTS + 32 * KB, F32R)
        proj = at("proj", [N_PROJ, S], REG)
        x1t = at("x1t", [KT, S], REG)
        hid_hi = at("hid_hi", [KT, S], REG + 32 * KB, F32R)
        hid_lo = at("hid_lo", [KT, S], REG + 64 * KB, F32R)
        w_raw = at("w_raw", [2, KT, P], WTS)
        w_hi = at("w_hi", [2, KT, P], WTS + 8 * KB, F32R)
        w_lo = at("w_lo", [2, KT, P], WTS + 16 * KB, F32R)
        cst = at("cst", [C_W], TMP)
        o = TMP + C_W * 4
        small = {}
        for name, n in (("vec", V_ROWS), ("ct", KT), ("ada", 48), ("a1", KT), ("a2", KT), ("qg8", 1), ("eps", 1),
                        ("ss", NB), ("sd", NB), ("rs", NB), ("sink", NQ), ("nsink", NQ)):
            small[name] = at(name, [n], o)
            o += (n * 4 + 31) // 32 * 32
        for name, n, m in (("mx", 3, 4), ("nm", 3, 4), ("es", 3, 4), ("ex", 3, 4), ("den", 3, 4), ("rd", 3, 4)):
            small[name] = at(name, [n, m], o)
            o += (n * m * 4 + 31) // 32 * 32
        r = REG + 88 * KB
        for name, n, m in (("bn", 2 * RH, 6), ("mv", 2 * RH, 2), ("rsd", 2, RH), ("rri", 2, RH), ("nmr", 2, RH)):
            small[name] = at(name, [n, m], r)
            r += (n * m * 4 + 31) // 32 * 32
        vec, ct, ada, a1, a2, qg8, eps, ss, sd8, rs8, sink, nsink = (
            small[k] for k in ("vec", "ct", "ada", "a1", "a2", "qg8", "eps", "ss", "sd", "rs", "sink", "nsink"))
        mx, nm, es, ex, den, rd, bn, mv, rsd, rri, nmr = (
            small[k] for k in ("mx", "nm", "es", "ex", "den", "rd", "bn", "mv", "rsd", "rri", "nmr"))
        TMPB = o
        assert TMPB + 16 * KB <= 229368, (TMPB + 16 * KB - 229368)

        xin = at("xin", [2, D], REG)
        rinv1 = at("rinv1", [S], REG + 8 * KB)
        ht1 = at("ht1", [2, HALF], REG + 12 * KB)
        wada1 = at("wada1", [3, 2 * D], REG + 16 * KB)
        xt = at("xt", [KT, S], REG + 40 * KB)
        acc = at("acc", [4 * D], REG + 72 * KB)
        wada2 = at("wada2", [2, D], REG + 88 * KB)
        diag = at("diag", [NB, P], TMPB)
        sqj = at("sqj", [2, D], TMPB + 4 * KB)
        vrow = at("vrow", [P], TMPB + 12 * KB)
        sqb = at("sqb", [2, HALF], TMPB)
        sdq = at("sdq", [2, HALF], TMPB + 4 * KB)
        riq = at("riq", [2, HALF], TMPB + 8 * KB)
        pr = [at("pr0", [GQA, 2 * P], REG + 88 * KB), at("pr1", [GQA, 2 * P], REG + 92 * KB),
              at("pr2", [GQA, 2 * P], TMPB)]
        prt = [at("prt0", [2, GQA * P], TMPB + 4 * KB), at("prt1", [2, GQA * P], TMPB + 8 * KB)]
        vnat = at("vnat", [NB, P], TMPB + 12 * KB)
        kdn = [at(f"kdn{i}", [RH, P], REG + (2 * i) * KB) for i in range(2)]
        rvn = [at(f"rvn{i}", [RH, P], REG + (4 + 2 * i) * KB) for i in range(2)]
        qd = [at(f"qd{i}", [RH, P], REG + (8 + 2 * i) * KB) for i in range(2)]
        inn = [at(f"inn{i}", [RH, P], REG + (12 + 2 * i) * KB) for i in range(2)]
        st = [at(f"st{i}", [RH, P], REG + (16 + 2 * i) * KB) for i in range(2)]
        onr = [at(f"onr{i}", [RH, P], REG + (20 + 2 * i) * KB) for i in range(2)]
        rvl = [at(f"rvl{i}", [RH, P], TMPB + 2 * i * KB) for i in range(2)]
        sq2 = at("sq2", [S], REG + 32 * KB)
        sqa = at("sqa", [S], REG + 36 * KB)
        sd2 = at("sd2", [S], REG + 40 * KB)
        rinv2 = at("rinv2", [S], REG + 44 * KB)
        ht2 = at("ht2", [2, HALF], REG + 48 * KB)
        rel = at("rel", [S], TMPB)
        rsq = at("rsq", [S], TMPB + 4 * KB)
        fin = at("fin", [S], TMPB + 8 * KB)
        ost = at("ost", [NB, P], TMPB + 12 * KB)

        ps = ctx.enter_context(nc.psum_tensor("ps", [P, 8, HALF], F32))
        ident = cst[:, C_ID:C_ID + P]
        ones = cst[:, C_ONE:C_ONE + P]
        blk = cst[:, C_BLK:C_BLK + P]
        dist = cst[:, C_DIST:C_DIST + 2 * P]

        def bank_pair(slot):
            return ps[:, 2 * slot:2 * slot + 2, :].rearrange("p a b -> p (a b)")

        def sem(name):
            return ctx.enter_context(nc.semaphore(name))

        s_cst, s_vrow, s_sink = sem("consts_loaded"), sem("vectors_loaded"), sem("sinks_loaded")
        s_xin = [sem("x_loaded_0"), sem("x_loaded_1")]
        s_wada1 = [sem(f"w_ada1_loaded_{i}") for i in range(3)]
        s_wada2 = [sem(f"w_ada2_loaded_{i}") for i in range(2)]
        s_raw = [sem("raw_loaded_0"), sem("raw_loaded_1")]
        s_spill, s_back, s_out = sem("x_spilled"), sem("x_back"), sem("out_stored")
        s_whi, s_wlo, s_mm, s_ev = sem("w_hi_ready"), sem("w_lo_ready"), sem("product_done"), sem("product_evacuated")
        s_vt, s_vec, s_ct = sem("vec_transposed"), sem("vec_ready"), sem("c_act_ready")
        s_xtp, s_xt, s_ssq, s_sd = sem("x_transposed"), sem("xt_ready"), sem("x_squares"), sem("x_sd")
        s_diag, s_bc = sem("diag_ready"), sem("rinv1_broadcast")
        s_rinv = sem("rinv_ready")
        s_acc, s_adat, s_ada = sem("ada_partial_done"), sem("ada_summed"), sem("ada_ready")
        s_h, s_hhi, s_act = sem("normed"), sem("normed_hi"), sem("operand_ready")
        s_dve = sem("vector_step")
        s_sqb, s_qss, s_sdq, s_riq, s_qn = sem("qk_squares"), sem("qk_sums"), sem("qk_sd"), sem("qk_rms_inverse"), sem("qk_normed")
        s_gate = sem("ret_gate_ready")
        s_vtr, s_vn = sem("v_transposed"), sem("v_natural")
        s_sc, s_add, s_nm, s_exp, s_pn = (sem("scores_done"), sem("scores_biased"), sem("neg_max_ready"),
                                          sem("exp_done"), sem("probs_ready"))
        s_pt, s_pe, s_pv = sem("probs_transposed"), sem("probs_t_ready"), sem("attention_done")
        s_mhi, s_mix = sem("mixed_hi"), sem("mixed_ready")
        s_rt, s_rvn, s_kdn = sem("ret_kv_transposed"), sem("ret_v_natural"), sem("ret_k_natural")
        s_in, s_inn, s_qd = sem("inner_done"), sem("inner_decayed"), sem("q_decayed")
        s_o, s_kv, s_st = sem("ret_out_done"), sem("ret_kv_done"), sem("state_ready")
        s_var, s_rsd, s_nmr, s_on = sem("ret_var"), sem("ret_sd"), sem("ret_norm_terms"), sem("ret_normed")
        s_ot, s_rvl = sem("ret_transposed"), sem("ret_gated")
        s_x1, s_sq2, s_sqa, s_ss2, s_sd2 = sem("x1_ready"), sem("x1_squares"), sem("x1_squares_summed"), sem("x1_sums"), sem("x1_sd")
        s_rel, s_rsq, s_hih, s_hid = sem("relu_done"), sem("relu_squared"), sem("hidden_hi"), sem("hidden_ready")
        s_ftr, s_ost = sem("final_transposed"), sem("out_staged")

        block = ctx.enter_context(nc.Block())

        def wait(eng, s, v):
            if not isinstance(v, int) or v > 0:
                eng.wait_ge(s, v)

        def loaded(t):
            return 16 * sum(2 if v < GQA else 3 if T_OUT <= v < T_MLP else 1 for v in range(t % 2, t + 1, 2))

        def pairs(eng, t0, n, step):
            first, second = loaded(t0 + 1), loaded(t0 + 2)
            if n > 1:
                per = (loaded(t0 + 3) - first) if n > 2 else 0
                assert n <= 2 or per == loaded(t0 + 4) - second
                assert n <= 2 or loaded(t0 + 2 * n - 2) == second + per * (n - 2)
                with eng.Fori(0, n - 1) as i:
                    step(i * 2 + t0, 0, i * per + first)
                    step(i * 2 + (t0 + 1), 1, i * per + second)
            for s in range(2):
                t = t0 + 2 * n - 2 + s
                step(t, s, loaded(t + 1) if t + 1 < N_TILES else None)

        @block.sync
        def _(sp):
            sp.dma_start(vrow[V_C:V_C + KT, :], c.rearrange("b (t p) -> (b t) p", p=P)).then_inc(s_vrow, 16)
            sp.dma_start(vrow[V_BADA:V_BADA + 48, :], b_ada.rearrange("l (t p) -> (l t) p", p=P)).then_inc(s_vrow, 16)
            sp.dma_start(vrow[V_N1:V_N1 + KT, :], norm1_g.rearrange("l (t p) -> (l t) p", p=P)).then_inc(s_vrow, 16)
            sp.dma_start(vrow[V_N2:V_N2 + KT, :], norm2_g.rearrange("l (t p) -> (l t) p", p=P)).then_inc(s_vrow, 16)
            sp.dma_start(vrow[V_RET:V_RET + RH, :], ret_norm_g.rearrange("l (t p) -> (l t) p", p=P)).then_inc(s_vrow, 16)
            for row, g in ((V_QG, q_norm_g), (V_KG, k_norm_g)):
                for half in range(2):
                    sp.dma_start(vrow[row:row + 1, half * HEAD:(half + 1) * HEAD], g).then_inc(s_vrow, 16)
            sp.dma_start(cst[:, :], consts).then_inc(s_cst, 16)
            sp.dma_start(sink[:, :], sinks[0].partition_broadcast(P)).then_inc(s_sink, 16)
            for n in range(NB):
                if n >= 2:
                    wait(sp, s_xtp, n - 1)
                    wait(sp, s_ssq, n - 1)
                sp.dma_start(xin[:, n % 2, :], x[0, n * P:(n + 1) * P, :]).then_inc(s_xin[n % 2], 16)

            w_in_k = w_in[0].rearrange("(k p) n -> p k n", p=P)
            w_in_q = w_in[0][:, 0:NQ * HEAD].rearrange("(k p) (g n) -> p k g n", p=P, g=NKV)

            def load(slot, src):
                sp.dma_start(w_raw[:, slot, :, :], src).then_inc(s_raw[slot], 16)

            for t in range(GQA):
                wait(sp, s_wlo, t - 1)
                for g in range(NKV):
                    sp.dma_start(w_raw[:, t % 2, :, g * HEAD:(g + 1) * HEAD],
                                 w_in_q[:, :, g, t * HEAD:(t + 1) * HEAD]).then_inc(s_raw[t % 2], 16)
            with sp.Fori(0, (N_PROJ - GQA) // 2) as i:
                for s in range(2):
                    sp.wait_ge(s_wlo, i * 2 + (GQA + s - 1))
                    load(s, w_in_k[:, :, bass.ds(i * 256 + (GQA + s) * P, P)])
            w_out_q = w_out[0][0:NQ * HEAD, :].rearrange("(g k d) n -> g d k n", g=NKV, k=GQA)
            w_out_r = w_out[0][NQ * HEAD:, :].rearrange("(k p) n -> p k n", p=P)
            with sp.Fori(0, N_OUT // 2) as i:
                for s in range(2):
                    sp.wait_ge(s_wlo, i * 2 + (T_OUT + s - 1))
                    cols = bass.ds(i * 256 + s * P, P)
                    for g in range(NKV):
                        sp.dma_start(w_raw[g * HEAD:(g + 1) * HEAD, s, 0:GQA, :], w_out_q[g][:, :, cols]).then_inc(s_raw[s], 16)
                    sp.dma_start(w_raw[:, s, GQA:, :], w_out_r[:, :, cols]).then_inc(s_raw[s], 16)
            w1_k = w_mlp1[0].rearrange("(k p) n -> p k n", p=P)
            w2_k = w_mlp2[0].rearrange("(q k p) n -> p q k n", p=P, q=QUARTERS)
            for q in range(QUARTERS):
                t0 = T_MLP + q * 2 * KT
                with sp.Fori(0, KT // 2) as i:
                    for s in range(2):
                        sp.wait_ge(s_wlo, i * 2 + (t0 + s - 1))
                        load(s, w1_k[:, :, bass.ds(i * 256 + q * D + s * P, P)])
                with sp.Fori(0, KT // 2) as i:
                    for s in range(2):
                        sp.wait_ge(s_wlo, i * 2 + (t0 + KT + s - 1))
                        load(s, w2_k[:, q, :, bass.ds(i * 256 + s * P, P)])

        @block.gpsimd
        def _(pool):
            for k in range(KT):
                if k >= 3:
                    wait(pool, s_acc, k - 2)
                pool.dma_start(wada1[:, k % 3, :], w_ada[0, k * P:(k + 1) * P, 0:2 * D]).then_inc(s_wada1[k % 3], 16)
            wait(pool, s_xt, NB)
            pool.dma_start(x_spill.rearrange("k p s -> p k s"), xt[:, :, :]).then_inc(s_spill, 16)
            for j in range(4):
                for k in range(KT):
                    u = j * KT + k
                    if u >= 2:
                        wait(pool, s_acc, KT + u - 1)
                    pool.dma_start(wada2[:, u % 2, :],
                                   w_ada[0, k * P:(k + 1) * P, (2 + j) * D:(3 + j) * D]).then_inc(s_wada2[u % 2], 16)
            wait(pool, s_spill, 16)
            for n in range(NB):
                if n == 0:
                    wait(pool, s_pv, NB)
                    wait(pool, s_ev, RQ + RH)
                if n >= 2:
                    wait(pool, s_o, n - 1)
                pool.tensor_tensor(qd[n % 2][:, :, :], proj[:, RQ:RQ + RH, n * P:(n + 1) * P],
                                   cst[:, C_QDEC:C_QDEC + RH * P].rearrange("p (h n) -> p h n", h=RH),
                                   ALU.mult).then_inc(s_qd, 1)
            wait(pool, s_o, NB)
            wait(pool, s_ot, NB)
            wait(pool, s_rvl, NB)
            wait(pool, s_qd, NB)
            wait(pool, s_on, NB)
            pool.dma_start(x1t[:, :, :], x_spill.rearrange("k p s -> p k s")).then_inc(s_back, 16)
            out_t = out[0].rearrange("(b p) n -> p b n", p=P)
            with pool.Fori(0, KT) as m:
                pool.wait_ge(s_ost, m + 1)
                pool.dma_start(out_t[:, :, bass.ds(m * P, P)], ost[:, :, :]).then_inc(s_out, 16)
            pool.wait_ge(s_out, 16 * KT)

        @block.tensor
        def _(pe):
            def product(t, slot, hi, lo, parts=None):
                pe.wait_ge(s_wlo, t + 1)
                wait(pe, s_ev, t - 1)
                for half in range(2):
                    bank = ps[:, 2 * slot + half, :]
                    cols = slice(half * HALF, (half + 1) * HALF)
                    for k in range(KT):
                        if parts is not None:
                            parts(half, k)
                        pe.matmul(bank, w_hi[:, slot, k, :], hi[:, k, cols], start=(k == 0), stop=False)
                        pe.matmul(bank, w_hi[:, slot, k, :], lo[:, k, cols], start=False, stop=False)
                        mm = pe.matmul(bank, w_lo[:, slot, k, :], hi[:, k, cols], start=False, stop=(k == KT - 1))
                mm.then_inc(s_mm, 1)

            pe.wait_ge(s_vrow, 16 * 9)
            pe.wait_ge(s_cst, 16)
            pe.transpose(ps[:, 7, 0:V_ROWS], vrow[0:V_ROWS, :], cst[0:V_ROWS, C_ID:C_ID + V_ROWS]).then_inc(s_vt, 1)
            for n in range(NB):
                pe.wait_ge(s_xin[n % 2], 16 * (n // 2 + 1))
                wait(pe, s_xt, n - 1)
                for k in range(KT):
                    tr = pe.transpose(ps[:, 2 * (n % 2) + k // 4, (k % 4) * P:(k % 4 + 1) * P],
                                      xin[:, n % 2, k * P:(k + 1) * P], ident)
                tr.then_inc(s_xtp, 1)
            pe.wait_ge(s_diag, 1)
            for half in range(2):
                mm = pe.matmul(ps[:, 4 + half, :], ones, diag[:, 4 * half:4 * half + 4, :].rearrange("p a b -> p (a b)"),
                               start=True, stop=True)
            mm.then_inc(s_bc, 1)

            def ada_sum(first, count):
                for m in range(count * KT):
                    mm = pe.matmul(ps[:, 6, 2 * m:2 * m + 2], acc[:, m * P:(m + 1) * P], cst[:, C_ONE:C_ONE + 2],
                                   start=True, stop=True)
                mm.then_inc(s_adat, 1)

            pe.wait_ge(s_acc, KT)
            ada_sum(0, 2)
            product(0, 0, act_hi, act_lo, lambda half, k: pe.wait_ge(s_act, half * KT + k + 1))
            product(1, 1, act_hi, act_lo)
            with pe.Fori(0, 8) as i:
                for s in range(2):
                    product(i * 2 + (2 + s), s, act_hi, act_lo)
            for u in range(10):
                pe.wait_ge(s_sqb, u + 1)
                wait(pe, s_sdq, u - 1)
                pe.matmul(ps[:, 4 + u % 2, :], blk, sqb[:, u % 2, :], start=True, stop=True).then_inc(s_qss, 1)
            pe.wait_ge(s_acc, KT + 4 * KT)
            pe.wait_ge(s_ada, 1)
            ada_sum(2, 4)
            with pe.Fori(0, 2) as i:
                for s in range(2):
                    product(i * 2 + (RG + s), s, act_hi, act_lo)

            pe.wait_ge(s_ev, N_PROJ)
            pe.wait_ge(s_qn, 10)
            for n in range(NB):
                tr = pe.transpose(ps[:, 6 + n // 4, (n % 4) * P:(n % 4 + 1) * P], proj[:, TV, n * P:(n + 1) * P], ident)
            tr.then_inc(s_vtr, 1)

            def scores(u):
                n, g = divmod(u, NKV)
                rows = slice(g * HEAD, (g + 1) * HEAD)
                lo = 0 if n else P
                wait(pe, s_add, u - 1)
                for p in range(GQA):
                    mm = pe.matmul(ps[:, 2 * (u % 2) + p // 2, (p % 2) * 256 + lo:(p % 2) * 256 + 256],
                                   proj[rows, TQ + p, n * P:(n + 1) * P],
                                   proj[rows, TK, (n - 1) * P + lo:(n + 1) * P], start=True, stop=True)
                mm.then_inc(s_sc, 1)

            scores(0)
            scores(1)
            pe.wait_ge(s_vn, 1)
            for u in range(NB * NKV):
                n, g = divmod(u, NKV)
                blocks = (0, 1) if n else (1,)
                pe.wait_ge(s_pn, u + 1)
                wait(pe, s_pe, u)
                for b in blocks:
                    for p in range(GQA):
                        tr = pe.transpose(ps[:, 4 + b, p * P:(p + 1) * P], pr[u % 3][:, p, b * P:(b + 1) * P], ident)
                tr.then_inc(s_pt, 1)
                if u + 2 < NB * NKV:
                    scores(u + 2)
                pe.wait_ge(s_pe, u + 1)
                if n >= 2:
                    pe.wait_ge(s_mix, n - 1)
                for b in blocks:
                    mm = pe.matmul(ps[g * HEAD:(g + 1) * HEAD, 6 + n % 2, :], vnat[:, n - 1 + b, g * HEAD:(g + 1) * HEAD],
                                   prt[u % 2][:, b, :], start=(b == blocks[0]), stop=(b == 1))
                if g == 1:
                    mm.then_inc(s_pv, 1)

            def ret_in(n):
                tok = slice(n * P, (n + 1) * P)
                wait(pe, s_kdn, n)
                wait(pe, s_rvn, n)
                for h in range(RH):
                    pe.transpose(ps[:, 0, h * P:(h + 1) * P], proj[:, RK + h, tok], ident)
                for h in range(RH):
                    tr = pe.transpose(ps[:, 1, h * P:(h + 1) * P], proj[:, RV + h, tok], ident)
                tr.then_inc(s_rt, 1)
                wait(pe, s_inn, n - 1)
                for h in range(RH):
                    mm = pe.matmul(ps[:, 2 + n % 2, h * P:(h + 1) * P], proj[:, RK + h, tok], proj[:, RQ + h, tok],
                                   start=True, stop=True)
                mm.then_inc(s_in, 1)

            def ret_out(n):
                if n + 1 < NB:
                    pe.wait_ge(s_kdn, n + 1)
                    pe.wait_ge(s_rvn, n + 1)
                    wait(pe, s_st, n)
                    for h in range(RH):
                        mm = pe.matmul(ps[:, 6, h * P:(h + 1) * P], kdn[n % 2][:, h, :], rvn[n % 2][:, h, :],
                                       start=True, stop=True)
                    mm.then_inc(s_kv, 1)
                pe.wait_ge(s_rvn, n + 1)
                pe.wait_ge(s_inn, n + 1)
                pe.wait_ge(s_qd, n + 1)
                wait(pe, s_on, n - 1)
                if n:
                    pe.wait_ge(s_st, n)
                for h in range(RH):
                    bank = ps[:, 4 + n % 2, h * P:(h + 1) * P]
                    mm = pe.matmul(bank, inn[n % 2][:, h, :], rvn[n % 2][:, h, :], start=True, stop=(n == 0))
                    if n:
                        mm = pe.matmul(bank, qd[n % 2][:, h, :], st[n % 2][:, h, :], start=False, stop=True)
                mm.then_inc(s_o, 1)

            def ret_turn(n):
                pe.wait_ge(s_on, n + 1)
                wait(pe, s_rvl, n)
                for h in range(RH):
                    tr = pe.transpose(ps[:, 7, h * P:(h + 1) * P], onr[n % 2][:, h, :], ident)
                tr.then_inc(s_ot, 1)

            pe.wait_ge(s_mix, NB)
            pe.wait_ge(s_add, NB * NKV)
            ret_in(0)
            for n in range(NB):
                if n + 1 < NB:
                    ret_in(n + 1)
                ret_out(n)
                if n:
                    ret_turn(n - 1)
            ret_turn(NB - 1)

            pe.wait_ge(s_mix, 2 * NB)
            with pe.Fori(0, N_OUT // 2) as i:
                for s in range(2):
                    product(i * 2 + (T_OUT + s), s, act_hi, act_lo)
            pe.wait_ge(s_sqa, N_OUT)
            for half in range(2):
                pe.matmul(ps[:, 4 + half, :], ones, sqa[:, half * HALF:(half + 1) * HALF],
                          start=True, stop=True).then_inc(s_ss2, 1)
            for q in range(QUARTERS):
                t0 = T_MLP + q * 2 * KT
                if q == 0:
                    product(t0, 0, act_hi, act_lo, lambda half, k: pe.wait_ge(s_act, 2 * KT + half * KT + k + 1))
                    product(t0 + 1, 1, act_hi, act_lo)
                first = 1 if q == 0 else 0
                with pe.Fori(first, KT // 2) as i:
                    for s in range(2):
                        product(i * 2 + (t0 + s), s, act_hi, act_lo)
                product(t0 + KT, 0, hid_hi, hid_lo,
                        lambda half, k: pe.wait_ge(s_hid, q * KT + k + 1) if half == 0 else None)
                product(t0 + KT + 1, 1, hid_hi, hid_lo)
                if q < QUARTERS - 1:
                    with pe.Fori(1, KT // 2) as i:
                        for s in range(2):
                            product(i * 2 + (t0 + KT + s), s, hid_hi, hid_lo)

            def turn(m):
                pe.wait_ge(s_ev, m + (N_TILES - KT + 1))
                wait(pe, s_ost, m)
                for n in range(NB):
                    tr = pe.transpose(ps[:, 4 + n // 4, (n % 4) * P:(n % 4 + 1) * P], fin[:, n * P:(n + 1) * P], ident)
                tr.then_inc(s_ftr, 1)

            turn(0)
            with pe.Fori(1, KT // 2) as i:
                for s in range(2):
                    product(i * 2 + (t0 + KT + s), s, hid_hi, hid_lo)
                    turn(i * 2 + (s - 1))
            turn(KT - 1)

        @block.scalar
        def _(act):
            def split_hi(t, slot, count):
                if count is None:
                    return
                act.wait_ge(s_raw[slot], count)
                wait(act, s_mm, t - 1)
                act.activation(w_hi[:, slot, :, :], w_raw[:, slot, :, :], ACT.Copy).then_inc(s_whi, 1)

            act.wait_ge(s_vec, 1)
            act.activation(ct[:, :], vec[:, V_C:V_C + KT], ACT.Silu).then_inc(s_ct, 1)
            for n in range(NB):
                act.wait_ge(s_xin[n % 2], 16 * (n // 2 + 1))
                if n >= 2:
                    act.wait_ge(s_ssq, n - 1)
                act.activation(sqj[:, n % 2, :], xin[:, n % 2, :], ACT.Square, accum_out=ss[:, n:n + 1]).then_inc(s_ssq, 1)
                act.wait_ge(s_xtp, n + 1)
                act.activation(xt[:, :, n * P:(n + 1) * P],
                               bank_pair(n % 2).rearrange("p (k n) -> p k n", k=KT), ACT.Copy).then_inc(s_xt, 1)
            act.wait_ge(s_ssq, NB)
            act.activation(sd8[:, :], ss[:, :], ACT.Sqrt, bias=eps[:, :], scale=1.0 / D).then_inc(s_sd, 1)
            act.wait_ge(s_bc, 1)
            act.activation(rinv1[:, :], ps[:, 4:6, :].rearrange("p a b -> p (a b)"), ACT.Copy).then_inc(s_rinv, 1)
            split_hi(0, 0, loaded(0))

            def norm_hi(shift, ht, base):
                for half in range(2):
                    for k in range(KT):
                        u = half * KT + k
                        act.wait_ge(s_h, base + u + 1)
                        act.activation(act_hi[:, k, half * HALF:(half + 1) * HALF], ht[:, u % 2, :], ACT.Identity,
                                       bias=ada[:, shift * KT + k:shift * KT + k + 1]).then_inc(s_hhi, 1)

            act.wait_ge(s_ada, 1)
            norm_hi(0, ht1, 0)

            def copy_out(func):
                def step(t, slot, count):
                    split_hi(t + 1, 1 - slot, count)
                    act.wait_ge(s_mm, t + 1)
                    act.activation(proj[:, bass.ds(t, 1), :].rearrange("p a s -> p (a s)"), bank_pair(slot),
                                   func).then_inc(s_ev, 1)
                return step

            for t in range(6):
                copy_out(ACT.Copy)(t, t % 2, loaded(t + 1))
            pairs(act, 6, 2, copy_out(ACT.Copy))
            act.wait_ge(s_spill, 16)
            pairs(act, 10, 4, copy_out(ACT.Copy))
            def qk_sd(u):
                act.wait_ge(s_qss, u + 1)
                wait(act, s_riq, u - 1)
                act.activation(sdq[:, u % 2, :], ps[:, 4 + u % 2, :], ACT.Sqrt, bias=eps[:, :],
                               scale=1.0 / HEAD).then_inc(s_sdq, 1)

            act.wait_ge(s_ev, 6)
            for u in range(10):
                t, half = divmod(u, 2)
                wait(act, s_qss, u - 1)
                act.activation(sqb[:, u % 2, :], proj[:, t, half * HALF:(half + 1) * HALF], ACT.Square).then_inc(s_sqb, 1)
                if u:
                    qk_sd(u - 1)
            qk_sd(9)
            act.wait_ge(s_adat, 2)
            pairs(act, RG, 2, copy_out(ACT.Silu))

            act.wait_ge(s_vtr, 1)
            act.activation(vnat[:, :, :].rearrange("p a b -> p (a b)"), ps[:, 6:8, :].rearrange("p a b -> p (a b)"),
                           ACT.Copy).then_inc(s_vn, 1)
            NU = NB * NKV

            def exps(u):
                lo = 0 if u >= NKV else P
                act.wait_ge(s_nm, u + 1)
                for p in range(GQA):
                    act.activation(pr[u % 3][:, p, lo:], pr[u % 3][:, p, lo:], ACT.Exp, bias=nm[:, u % 3, p:p + 1],
                                   accum_out=den[:, u % 3, p:p + 1])
                act.activation(ex[:, u % 3, :], es[:, u % 3, :], ACT.Exp).then_inc(s_exp, 1)

            def attn_hi(n):
                act.wait_ge(s_pv, n + 1)
                act.activation(act_hi[:, 0:GQA, n * P:(n + 1) * P], ps[:, 6 + n % 2, :].rearrange("p (k n) -> p k n", k=GQA),
                               ACT.Copy).then_inc(s_mhi, 1)

            exps(0)
            exps(1)
            for u in range(NU):
                b0 = 0 if u >= NKV else 1
                act.wait_ge(s_pt, u + 1)
                act.activation(prt[u % 2][:, b0:, :], ps[:, 4 + b0:6, :], ACT.Copy).then_inc(s_pe, 1)
                if u >= NKV and u % NKV == 0:
                    attn_hi(u // NKV - 1)
                if u + 2 < NU:
                    exps(u + 2)
            attn_hi(NB - 1)

            def ret_v(n):
                act.wait_ge(s_rt, n + 1)
                wait(act, s_o, n - 1)
                act.activation(rvn[n % 2][:, :, :].rearrange("p a b -> p (a b)"), ps[:, 1, :], ACT.Copy).then_inc(s_rvn, 1)

            def ret_hi(n):
                act.wait_ge(s_rvl, n + 1)
                act.activation(act_hi[:, GQA:, n * P:(n + 1) * P], rvl[n % 2][:, :, :], ACT.Copy).then_inc(s_mhi, 1)

            ret_v(0)
            for n in range(NB):
                if n + 1 < NB:
                    ret_v(n + 1)
                act.wait_ge(s_var, n + 1)
                act.activation(rsd[:, n % 2, :], mv[:, (n % 2) * RH:(n % 2 + 1) * RH, 1], ACT.Sqrt,
                               bias=eps[:, :]).then_inc(s_rsd, 1)
                if n:
                    ret_hi(n - 1)
                act.wait_ge(s_nmr, n + 1)
                wait(act, s_ot, n - 1)
                for h in range(RH):
                    on = act.activation(onr[n % 2][:, h, :], ps[:, 4 + n % 2, h * P:(h + 1) * P], ACT.Identity,
                                        bias=nmr[:, n % 2, h:h + 1], scale=rri[:, n % 2, h:h + 1])
                on.then_inc(s_on, 1)
            ret_hi(NB - 1)

            def square_x1(t, slot, count):
                split_hi(t + 1, 1 - slot, count)
                m = t - T_OUT
                act.wait_ge(s_ev, t + 1)
                wait(act, s_sqa, m)
                act.activation(sq2[:, :], x1t[:, bass.ds(m, 1), :].rearrange("p a s -> p (a s)"),
                               ACT.Square).then_inc(s_sq2, 1)

            split_hi(T_OUT, 0, None)
            square_x1(T_OUT, 0, loaded(T_OUT + 1))
            square_x1(T_OUT + 1, 1, loaded(T_OUT + 2))
            pairs(act, T_OUT + 2, N_OUT // 2 - 1, square_x1)
            for half in range(2):
                act.wait_ge(s_ss2, half + 1)
                cols = slice(half * HALF, (half + 1) * HALF)
                act.activation(sd2[:, cols], ps[:, 4 + half, :], ACT.Sqrt, bias=eps[:, :], scale=1.0 / D).then_inc(s_sd2, 1)
            norm_hi(3, ht2, 2 * KT)

            for q in range(QUARTERS):
                t0 = T_MLP + q * 2 * KT

                def up(t, slot, count, t0=t0, q=q):
                    split_hi(t + 1, 1 - slot, count)
                    m = t - t0
                    act.wait_ge(s_mm, t + 1)
                    wait(act, s_rsq, m + q * KT)
                    act.activation(rel[:, :], bank_pair(slot), ACT.Relu).then_inc(s_ev, 1)
                    act.wait_ge(s_rsq, m + (q * KT + 1))
                    act.activation(hid_hi[:, bass.ds(m, 1), :].rearrange("p a s -> p (a s)"), rsq[:, :],
                                   ACT.Copy).then_inc(s_hih, 1)

                def down(t, slot, count):
                    split_hi(t + 1, 1 - slot, count)

                if q == 0:
                    up(t0, 0, loaded(t0 + 1))
                    up(t0 + 1, 1, loaded(t0 + 2))
                    pairs(act, t0 + 2, KT // 2 - 1, up)
                else:
                    pairs(act, t0, KT // 2, up)
                if q < QUARTERS - 1:
                    pairs(act, t0 + KT, KT // 2, down)
            def stage(m):
                act.wait_ge(s_ftr, m + 1)
                wait(act, s_out, m * 16)
                act.activation(ost[:, :, :].rearrange("p a b -> p (a b)"), ps[:, 4:6, :].rearrange("p a b -> p (a b)"),
                               ACT.Copy).then_inc(s_ost, 1)

            t0 = N_TILES - KT
            down(t0, 0, loaded(t0 + 1))
            down(t0 + 1, 1, loaded(t0 + 2))
            stage(0)

            def down_last(t, slot, count):
                down(t, slot, count)
                stage(t - (t0 + 1))

            pairs(act, t0 + 2, KT // 2 - 1, down_last)
            stage(KT - 1)

        @block.vector
        def _(dve):
            own = [0]

            def link(ins):
                own[0] += 1
                ins.then_inc(s_dve, 1)
                dve.wait_ge(s_dve, own[0])

            def split_lo(t, slot, count=0):
                if count is None:
                    return
                dve.wait_ge(s_whi, t + 1)
                dve.tensor_tensor(w_lo[:, slot, :, :], w_raw[:, slot, :, :], w_hi[:, slot, :, :].bitcast(F32),
                                  ALU.subtract).then_inc(s_wlo, 1)

            dve.memset(eps[:, :], EPS).then_inc(s_dve, 1)
            own[0] += 1
            dve.wait_ge(s_vt, 1)
            dve.tensor_copy(vec[:, :], ps[:, 7, 0:V_ROWS]).then_inc(s_vec, 1)
            dve.wait_ge(s_vec, 1)
            dve.wait_ge(s_sink, 16)
            link(dve.tensor_scalar(qg8[:, :], vec[:, V_QG:V_QG + 1], HEAD ** -0.5, None, ALU.mult))
            link(dve.tensor_scalar(nsink[:, :], sink[:, :], -1.0, None, ALU.mult))
            dve.wait_ge(s_ct, 1)
            for k in range(KT):
                dve.wait_ge(s_wada1[k % 3], 16 * (k // 3 + 1))
                if k == 0:
                    dve.tensor_scalar(acc[:, 0:2 * D], wada1[:, 0, :], ct[:, 0:1], None, ALU.mult).then_inc(s_acc, 1)
                else:
                    dve.wait_ge(s_acc, k)
                    dve.scalar_tensor_tensor(out=acc[:, 0:2 * D], in0=wada1[:, k % 3, :], scalar=ct[:, k:k + 1],
                                             in1=acc[:, 0:2 * D], op0=ALU.mult, op1=ALU.add).then_inc(s_acc, 1)
                if k == 5:
                    dve.wait_ge(s_sd, 1)
                    link(dve.reciprocal(rs8[:, :], sd8[:, :]))
                    for n in range(NB):
                        dg = dve.tensor_scalar(diag[:, n, :], ident, rs8[:, n:n + 1], None, ALU.mult)
                    dg.then_inc(s_diag, 1)
            split_lo(0, 0)

            def ada_columns(j, first):
                src = ps[:, 6, 16 * (j - first):16 * (j - first) + 16].rearrange("p (m two) -> p m two", two=2)[:, :, 0]
                dst = ada[:, j * KT:(j + 1) * KT]
                bias = vec[:, V_BADA + j * KT:V_BADA + (j + 1) * KT]
                if j in (1, 4):
                    link(dve.scalar_tensor_tensor(out=dst, in0=src, scalar=1.0, in1=bias, op0=ALU.add, op1=ALU.add))
                    gain, a = ((V_N1, a1), (V_N2, a2))[j == 4]
                    return dve.tensor_tensor(a[:, :], dst, vec[:, gain:gain + KT], ALU.mult)
                return dve.tensor_tensor(dst, src, bias, ALU.add)

            dve.wait_ge(s_adat, 1)
            link(ada_columns(0, 0))
            ada_columns(1, 0).then_inc(s_ada, 1)
            dve.wait_ge(s_ada, 1)

            def normed(src, scale, shift, rinv, ht, base):
                def low(u):
                    half, k = divmod(u, KT)
                    cols = slice(half * HALF, (half + 1) * HALF)
                    dve.wait_ge(s_hhi, base + u + 1)
                    dve.scalar_tensor_tensor(out=act_lo[:, k, cols], in0=ht[:, u % 2, :],
                                             scalar=ada[:, shift * KT + k:shift * KT + k + 1],
                                             in1=act_hi[:, k, cols].bitcast(F32), op0=ALU.add,
                                             op1=ALU.subtract).then_inc(s_act, 1)

                for u in range(2 * KT):
                    half, k = divmod(u, KT)
                    cols = slice(half * HALF, (half + 1) * HALF)
                    if u >= 2:
                        dve.wait_ge(s_act, base + u - 1)
                    dve.scalar_tensor_tensor(out=ht[:, u % 2, :], in0=src[:, k, cols], scalar=scale[:, k:k + 1],
                                             in1=rinv[:, cols], op0=ALU.mult, op1=ALU.mult).then_inc(s_h, 1)
                    if u:
                        low(u - 1)
                low(2 * KT - 1)

            dve.wait_ge(s_xt, NB)
            dve.wait_ge(s_rinv, 1)
            normed(xt, a1, 0, rinv1, ht1, 0)

            def only_lo(t, slot, count):
                split_lo(t + 1, 1 - slot, count)

            pairs(dve, 0, 2, only_lo)
            pairs(dve, 4, 1, only_lo)
            with dve.Fori(0, 4) as j:
                col = acc[:, bass.ds(j * D, D)]
                for s in range(2):
                    split_lo(j * 2 + (7 + s), 1 - s)
                    for k in range(4 * s, 4 * s + 4):
                        dve.wait_ge(s_wada2[k % 2], j * 64 + (16 * (k // 2 + 1)))
                        if k == 0:
                            dve.tensor_scalar(col, wada2[:, 0, :], ct[:, 0:1], None, ALU.mult).then_inc(s_acc, 1)
                        else:
                            dve.wait_ge(s_acc, j * KT + (KT + k))
                            dve.scalar_tensor_tensor(out=col, in0=wada2[:, k % 2, :], scalar=ct[:, k:k + 1], in1=col,
                                                     op0=ALU.mult, op1=ALU.add).then_inc(s_acc, 1)
            pairs(dve, 14, 2, only_lo)
            for u in range(10):
                t, half = divmod(u, 2)
                cols = slice(half * HALF, (half + 1) * HALF)
                gain = qg8[:, 0:1] if t < GQA else vec[:, V_KG:V_KG + 1]
                dve.wait_ge(s_sdq, u + 1)
                wait(dve, s_qn, u - 1)
                dve.reciprocal(riq[:, u % 2, :], sdq[:, u % 2, :]).then_inc(s_riq, 1)
                dve.wait_ge(s_riq, u + 1)
                dve.scalar_tensor_tensor(out=proj[:, t, cols], in0=proj[:, t, cols], scalar=gain, in1=riq[:, u % 2, :],
                                         op0=ALU.mult, op1=ALU.mult).then_inc(s_qn, 1)
            dve.wait_ge(s_adat, 2)
            for j in range(2, 6):
                link(ada_columns(j, 2))
            pairs(dve, RG, 2, only_lo)
            dve.wait_ge(s_ev, N_PROJ)
            for h in range(RH):
                dve.tensor_scalar(proj[:, RG + h, :], proj[:, RG + h, :], vec[:, V_RET + h:V_RET + h + 1], None,
                                  ALU.mult).then_inc(s_gate, 1)

            NU = NB * NKV

            def bias_max(u):
                g, i, lo = u % NKV, u % 3, 0 if u >= NKV else P
                dve.wait_ge(s_sc, u + 1)
                wait(dve, s_pt, u - 2)
                for p in range(GQA):
                    ad = dve.scalar_tensor_tensor(
                        out=pr[i][:, p, lo:], in0=dist[:, lo:], scalar=-SLOPES[g * GQA + p],
                        in1=ps[:, 2 * (u % 2) + p // 2, (p % 2) * 256 + lo:(p % 2) * 256 + 256], op0=ALU.mult, op1=ALU.add)
                ad.then_inc(s_add, 1)
                dve.wait_ge(s_add, u + 1)
                link(dve.tensor_reduce(mx[:, i, :], pr[i][:, :, lo:], AX_X, ALU.max))
                heads = slice(g * GQA, (g + 1) * GQA)
                link(dve.scalar_tensor_tensor(out=nm[:, i, :], in0=mx[:, i, :], scalar=-1.0, in1=nsink[:, heads],
                                              op0=ALU.mult, op1=ALU.min))
                dve.tensor_tensor(es[:, i, :], nm[:, i, :], sink[:, heads], ALU.add).then_inc(s_nm, 1)

            def normalise(u):
                i, lo = u % 3, 0 if u >= NKV else P
                dve.wait_ge(s_exp, u + 1)
                link(dve.tensor_tensor(den[:, i, :], den[:, i, :], ex[:, i, :], ALU.add))
                link(dve.reciprocal(rd[:, i, :], den[:, i, :]))
                for p in range(GQA):
                    pn = dve.tensor_scalar(pr[i][:, p, lo:], pr[i][:, p, lo:], rd[:, i, p:p + 1], None, ALU.mult)
                pn.then_inc(s_pn, 1)

            def attn_lo(n):
                dve.wait_ge(s_mhi, n + 1)
                tok = slice(n * P, (n + 1) * P)
                dve.tensor_tensor(act_lo[:, 0:GQA, tok], ps[:, 6 + n % 2, :].rearrange("p (k n) -> p k n", k=GQA),
                                  act_hi[:, 0:GQA, tok].bitcast(F32), ALU.subtract).then_inc(s_mix, 1)

            bias_max(0)
            bias_max(1)
            normalise(0)
            for u in range(NU):
                if u + 2 < NU:
                    bias_max(u + 2)
                if u + 1 < NU:
                    normalise(u + 1)
                if u >= NKV and u % NKV == 0:
                    attn_lo(u // NKV - 1)
            attn_lo(NB - 1)

            def ret_in(n):
                i = n % 2
                dve.wait_ge(s_rt, n + 1)
                wait(dve, s_o, n - 1)
                kdec = cst[:, C_KDEC:C_KDEC + RH].unsqueeze(2).broadcast_to([P, RH, P])
                dve.tensor_tensor(kdn[i][:, :, :], ps[:, 0, :].rearrange("p (h n) -> p h n", h=RH), kdec,
                                  ALU.mult).then_inc(s_kdn, 1)
                dve.wait_ge(s_in, n + 1)
                dve.tensor_tensor(inn[i][:, :, :].rearrange("p h n -> p (h n)"), ps[:, 2 + i, :],
                                  cst[:, C_DEC:C_DEC + RH * P], ALU.mult).then_inc(s_inn, 1)

            def ret_state(n):
                dve.wait_ge(s_kv, n + 1)
                wait(dve, s_o, n)
                new, old = st[(n + 1) % 2], st[n % 2]
                if n == 0:
                    dve.tensor_copy(new[:, :, :].rearrange("p h n -> p (h n)"), ps[:, 6, :]).then_inc(s_st, 1)
                    return
                dve.wait_ge(s_st, n)
                for h in range(RH):
                    up = dve.scalar_tensor_tensor(out=new[:, h, :], in0=old[:, h, :],
                                                  scalar=cst[:, C_CHUNK + h:C_CHUNK + h + 1],
                                                  in1=ps[:, 6, h * P:(h + 1) * P], op0=ALU.mult, op1=ALU.add)
                up.then_inc(s_st, 1)

            def ret_gate(n):
                i = n % 2
                dve.wait_ge(s_ot, n + 1)
                wait(dve, s_mix, NB + n - 1)
                dve.tensor_tensor(rvl[i][:, :, :], ps[:, 7, :].rearrange("p (h n) -> p h n", h=RH),
                                  proj[:, RG:RG + RH, n * P:(n + 1) * P], ALU.mult).then_inc(s_rvl, 1)

            def ret_lo(n):
                tok = slice(n * P, (n + 1) * P)
                dve.wait_ge(s_mhi, NB + n + 1)
                dve.tensor_tensor(act_lo[:, GQA:, tok], rvl[n % 2][:, :, :], act_hi[:, GQA:, tok].bitcast(F32),
                                  ALU.subtract).then_inc(s_mix, 1)

            dve.wait_ge(s_gate, RH)
            dve.wait_ge(s_pv, NB)
            ret_in(0)
            for n in range(NB):
                i = n % 2
                if n + 1 < NB:
                    ret_in(n + 1)
                    ret_state(n)
                dve.wait_ge(s_o, n + 1)
                if n >= 2:
                    dve.wait_ge(s_on, n - 1)
                for h in range(RH):
                    b = dve.bn_stats(bn[:, i * RH + h, :], ps[:, 4 + i, h * P:(h + 1) * P])
                link(b)
                for h in range(RH):
                    b = dve.bn_aggr(mv[:, i * RH + h, :], bn[:, i * RH + h, :])
                b.then_inc(s_var, 1)
                if n:
                    ret_gate(n - 1)
                dve.wait_ge(s_rsd, n + 1)
                dve.wait_ge(s_var, n + 1)
                link(dve.reciprocal(rri[:, i, :], rsd[:, i, :]))
                dve.scalar_tensor_tensor(out=nmr[:, i, :], in0=mv[:, i * RH:(i + 1) * RH, 0], scalar=-1.0, in1=rri[:, i, :],
                                         op0=ALU.mult, op1=ALU.mult).then_inc(s_nmr, 1)
                if n:
                    ret_lo(n - 1)
            ret_gate(NB - 1)
            ret_lo(NB - 1)

            def residual(gate, base, t, slot):
                m = t - base
                dve.wait_ge(s_mm, t + 1)
                tile = x1t[:, bass.ds(m, 1), :].rearrange("p a s -> p (a s)")
                dve.scalar_tensor_tensor(out=tile, in0=bank_pair(slot), scalar=ada[:, bass.ds(m + gate * KT, 1)],
                                         in1=tile, op0=ALU.mult, op1=ALU.add).then_inc(s_ev, 1)

            def out_step(t, slot, count):
                split_lo(t + 1, 1 - slot, count)
                residual(2, T_OUT, t, slot)
                m = t - T_OUT
                dve.wait_ge(s_sq2, m + 1)
                if isinstance(m, int) and m == 0:
                    dve.tensor_copy(sqa[:, :], sq2[:, :]).then_inc(s_sqa, 1)
                else:
                    dve.wait_ge(s_sqa, m)
                    dve.tensor_tensor(sqa[:, :], sqa[:, :], sq2[:, :], ALU.add).then_inc(s_sqa, 1)

            dve.wait_ge(s_back, 16)
            out_step(T_OUT, 0, 0)
            out_step(T_OUT + 1, 1, 0)
            pairs(dve, T_OUT + 2, N_OUT // 2 - 1, out_step)
            for half in range(2):
                cols = slice(half * HALF, (half + 1) * HALF)
                dve.wait_ge(s_sd2, half + 1)
                link(dve.reciprocal(rinv2[:, cols], sd2[:, cols]))
            normed(x1t, a2, 3, rinv2, ht2, 2 * KT)

            for q in range(QUARTERS):
                t0 = T_MLP + q * 2 * KT

                def up(t, slot, count, t0=t0, q=q):
                    split_lo(t + 1, 1 - slot, count)
                    m = t - t0
                    dve.wait_ge(s_ev, t + 1)
                    wait(dve, s_hid, m + q * KT)
                    dve.tensor_tensor(rsq[:, :], rel[:, :], rel[:, :], ALU.mult).then_inc(s_rsq, 1)
                    dve.wait_ge(s_hih, m + (q * KT + 1))
                    tile = bass.ds(m, 1)
                    dve.tensor_tensor(hid_lo[:, tile, :].rearrange("p a s -> p (a s)"), rsq[:, :],
                                      hid_hi[:, tile, :].bitcast(F32).rearrange("p a s -> p (a s)"),
                                      ALU.subtract).then_inc(s_hid, 1)

                def down(t, slot, count, t0=t0):
                    split_lo(t + 1, 1 - slot, count)
                    residual(5, t0 + KT, t, slot)

                if q == 0:
                    up(t0, 0, 0)
                    up(t0 + 1, 1, 0)
                    pairs(dve, t0 + 2, KT // 2 - 1, up)
                else:
                    pairs(dve, t0, KT // 2, up)
                if q < QUARTERS - 1:
                    pairs(dve, t0 + KT, KT // 2, down)

            def down_last(t, slot, count):
                split_lo(t + 1, 1 - slot, count)
                m = t - (N_TILES - KT)
                dve.wait_ge(s_mm, t + 1)
                wait(dve, s_ftr, m)
                dve.scalar_tensor_tensor(out=fin[:, :], in0=bank_pair(slot), scalar=ada[:, bass.ds(m + 5 * KT, 1)],
                                         in1=x1t[:, bass.ds(m, 1), :].rearrange("p a s -> p (a s)"),
                                         op0=ALU.mult, op1=ALU.add).then_inc(s_ev, 1)

            down_last(N_TILES - KT, 0, 0)
            down_last(N_TILES - KT + 1, 1, 0)
            pairs(dve, N_TILES - KT + 2, KT // 2 - 1, down_last)


_INS = ["x", "c", "norm1_g", "norm2_g", "w_ada", "b_ada", "w_in", "q_norm_g", "k_norm_g", "sinks", "ret_norm_g",
        "w_out", "w_mlp1", "w_mlp2"]


def kernel(**inputs):
    import numpy as np
    import concourse.bacc as bacc
    from concourse.bass_utils import run_bass_kernel_spmd as run

    nc = bacc.Bacc("TRN2", target_bir_lowering=False, num_devices=1)
    arrays, args = {}, []
    for name in _INS:
        a = np.ascontiguousarray(inputs[name])
        arrays[f"in_{name}_dram"] = a
        args.append(nc.dram_tensor(f"in_{name}_dram", a.shape, mybir.dt.from_np(a.dtype), kind="ExternalInput").ap())
    arrays["shape_constants"] = shape_constants()
    args.append(nc.dram_tensor("shape_constants", (P, C_W), F32, kind="ExternalInput").ap())
    args.append(nc.dram_tensor("x_spill", (KT, P, S), F32, kind="Internal").ap())
    args.append(nc.dram_tensor("out_0_dram", (1, S, D), F32, kind="ExternalOutput").ap())
    hybrid_layer(nc, *args)
    r = run(nc, [arrays], core_ids=[0])
    return r.results[0]["out_0_dram"]
```

```python
from contextlib import ExitStack

import concourse.bass as bass
from concourse import mybir

F32 = mybir.dt.float32
F32R = mybir.dt.float32r
ALU = mybir.AluOpType
ACT = mybir.ActivationFunctionType
AX_X = mybir.AxisListType.X

P = 128
D = 1024
S = 1024
KT = D // P
NB = S // P
HALF = 512
HEAD = 64
NQ, NKV = 8, 2
GQA = NQ // NKV
RH = 4
FF = 4 * D
EPS = 1e-6
IN_W = 2816
TK, TV, TQ, RQ, RK, RV, RG = 0, 1, 2, 6, 10, 14, 18
N_PROJ = IN_W // P
N_OUT = D // P
XS = 4
QUARTERS = 4
HK = KT // 2
T_A = N_PROJ
T_B = T_A + N_OUT
T_M = T_B + 2 * N_OUT
N_TILES = T_M + QUARTERS * 2 * KT
SLOPES = [2.0 ** (-8.0 * (h + 1) / NQ) for h in range(NQ)]
MASKED = 1e33
C_ID, C_ONE, C_BLK, C_DIST, C_DEC, C_QDEC, C_KDEC = 0, 128, 256, 384, 640, 1152, 1664
C_CHUNK = 1668
C_W = 1672
V_C, V_BADA, V_N1, V_N2, V_RET, V_QG, V_KG, V_ROWS = 0, 8, 56, 64, 72, 76, 77, 78


def shape_constants():
    import numpy as np

    c = np.zeros((P, C_W), np.float64)
    i = np.arange(P)
    c[:, C_ID:C_ID + P] = np.eye(P)
    c[:, C_ONE:C_ONE + P] = 1.0
    c[:, C_BLK:C_BLK + P] = (i[:, None] // HEAD) == (i[None, :] // HEAD)
    dist = i[:, None] + P - np.arange(2 * P)[None, :]
    c[:, C_DIST:C_DIST + 2 * P] = np.where((dist >= 0) & (dist < P), dist, MASKED)
    for h in range(RH):
        lg = np.log1p(-(2.0 ** (-5.0 - h)))
        rel = i[None, :] - i[:, None]
        c[:, C_DEC + h * P:C_DEC + (h + 1) * P] = np.where(rel >= 0, np.exp(lg * np.maximum(rel, 0)), 0) * P ** -0.5
        c[:, C_QDEC + h * P:C_QDEC + (h + 1) * P] = np.exp(lg * (i + 1.0))[None, :]
        c[:, C_KDEC + h] = np.exp(lg * (P - 1.0 - i)) * P ** -0.5
        c[:, C_CHUNK + h] = np.exp(lg * P)
    return c.astype(np.float32)


def hybrid_layer(nc, x, c, norm1_g, norm2_g, w_ada, b_ada, w_in, q_norm_g, k_norm_g, sinks,
                 ret_norm_g, w_out, w_mlp1, w_mlp2, consts, x_spill, out):
    ctx = ExitStack()
    with ctx:
        KB = 1024
        BASE = 16512
        ACTS, REG, WTS, TMP = BASE, BASE + 64 * KB, BASE + 160 * KB, BASE + 184 * KB

        def at(name, shape, off, dt=F32):
            return nc.alloc_sbuf_tensor_at(name, [P] + shape, dt, offset=off)

        act_hi = at("act_hi", [KT, S], ACTS, F32R)
        act_lo = at("act_lo", [KT, S], ACTS + 32 * KB, F32R)
        hn = at("hn", [KT, S], ACTS + 32 * KB)
        proj = at("proj", [N_PROJ, S], REG + 8 * KB)
        x1t = at("x1t", [KT, S], REG)
        hid_hi = at("hid_hi", [KT, S], REG + 32 * KB, F32R)
        hid_lo = at("hid_lo", [KT, S], REG + 64 * KB, F32R)
        w_raw = at("w_raw", [2, KT, P], WTS)
        w_hi = at("w_hi", [2, KT, P], WTS + 8 * KB, F32R)
        w_lo = at("w_lo", [2, KT, P], WTS + 16 * KB, F32R)
        cst = at("cst", [C_W], TMP)
        small = {}
        o = TMP + C_W * 4
        for name, *shape in (("vec", V_ROWS), ("ct", KT), ("ada", 6 * KT), ("a1", KT), ("a2", KT), ("qg8", 1), ("eps", 1),
                             ("ss", NB), ("sd8", NB), ("rs8", NB), ("sink", NQ), ("nsink", NQ),
                             ("mx", 2, 4), ("nm", 2, 4), ("es", 2, 4), ("ex", 2, 4), ("den", 2, 4), ("rd", 2, 4),
                             ("bn", RH, 6), ("mv", RH, 2), ("rsd", RH), ("rri", RH), ("nmr", RH)):
            small[name] = at(name, list(shape), o)
            o += (shape[0] * (shape[1] if len(shape) > 1 else 1) * 4 + 31) // 32 * 32
        vec, ct, ada, a1, a2, qg8, eps, ss, sd8, rs8, sink, nsink = (
            small[k] for k in ("vec", "ct", "ada", "a1", "a2", "qg8", "eps", "ss", "sd8", "rs8", "sink", "nsink"))
        mx, nm, es, ex, den, rd, bn, mv, rsd, rri, nmr = (
            small[k] for k in ("mx", "nm", "es", "ex", "den", "rd", "bn", "mv", "rsd", "rri", "nmr"))
        TMPB = o
        assert TMPB + 16 * KB <= 229368, TMPB + 16 * KB - 229368

        xin = at("xin", [XS, D], REG)
        xt = at("xt", [KT, S], REG + 44 * KB)
        acc = at("acc", [4 * D], REG + 80 * KB)
        wada1 = [at(f"wada1_{k}", [2 * D], off) for k, off in enumerate(
            [REG + (4 * XS + 8 * i) * KB for i in range(3)] + [REG + 88 * KB] + [ACTS + 8 * i * KB for i in range(4)])]
        wada2 = at("wada2", [2, D], REG)
        diag = at("diag", [NB, P], TMPB)
        sqj = at("sqj", [2, D], TMPB + 4 * KB)
        vrow = at("vrow", [P], TMPB + 12 * KB)
        sqb = at("sqb", [2, HALF], TMPB)
        sdq = at("sdq", [2, HALF], TMPB + 4 * KB)
        riq = at("riq", [2, HALF], TMPB + 8 * KB)
        pr = [at("pr0", [GQA, 2 * P], TMPB), at("pr1", [GQA, 2 * P], TMPB + 4 * KB)]
        prt = at("prt", [2, GQA * P], TMPB + 8 * KB)
        vnat = at("vnat", [NB, P], TMPB + 12 * KB)
        kdn = at("kdn", [RH, P], TMPB)
        rvn = at("rvn", [RH, P], TMPB + 2 * KB)
        inn = at("inn", [RH, P], TMPB + 4 * KB)
        qd = at("qd", [RH, P], TMPB + 6 * KB)
        st = [at(f"st{i}", [RH, P], TMPB + (8 + 2 * i) * KB) for i in range(2)]
        onr = at("onr", [RH, P], TMPB + 12 * KB)
        rvl = at("rvl", [RH, P], TMPB + 14 * KB)
        sq2 = at("sq2", [2, HALF], REG + 32 * KB)
        sqa = at("sqa", [2, HALF], REG + 36 * KB)
        sd2 = at("sd2", [2, HALF], REG + 40 * KB)
        rinv2 = at("rinv2", [2, HALF], REG + 44 * KB)
        ht2 = at("ht2", [2, HALF], REG + 48 * KB)
        rel = at("rel", [S], TMPB)
        rsq = at("rsq", [S], TMPB + 4 * KB)
        fin = at("fin", [S], TMPB + 8 * KB)
        ost = at("ost", [NB, P], TMPB + 12 * KB)

        ps = ctx.enter_context(nc.psum_tensor("ps", [P, 8, HALF], F32))
        ident = cst[:, C_ID:C_ID + P]
        ones = cst[:, C_ONE:C_ONE + P]
        blk = cst[:, C_BLK:C_BLK + P]
        dist = cst[:, C_DIST:C_DIST + 2 * P]
        HALVES = [slice(0, HALF), slice(HALF, S)]

        def flat(ap):
            return ap.rearrange("p a b -> p (a b)")

        def bank_pair(slot):
            return flat(ps[:, 2 * slot:2 * slot + 2, :])

        def tile_of(tensor, m):
            return flat(tensor[:, bass.ds(m, 1), :])

        def tokens(n):
            return slice(n * P, (n + 1) * P)

        def sem(name):
            return ctx.enter_context(nc.semaphore(name))

        s_cst, s_vrow, s_sink = sem("consts_loaded"), sem("vectors_loaded"), sem("sinks_loaded")
        s_c, s_id = sem("c_loaded"), sem("identity_loaded")
        s_xin = [sem(f"x_loaded_{n}") for n in range(NB)]
        s_wada1 = [sem(f"w_ada1_loaded_{k}") for k in range(KT)]
        s_wada2 = [sem(f"w_ada2_loaded_{i}") for i in range(2)]
        s_raw = [sem("raw_loaded_0"), sem("raw_loaded_1")]
        s_spill, s_out = sem("x_spilled"), sem("out_stored")
        s_back = [sem(f"x_back_{m}") for m in range(KT)]
        s_whi, s_wlo = sem("w_hi_ready"), sem("w_lo_ready")
        s_mmp, s_mma, s_mmb, s_mmm = (sem(n) for n in ("proj_done", "out_a_done", "out_b_done", "mlp_done"))
        s_evp, s_eva, s_evb, s_evm = (sem(n) for n in ("proj_stored", "out_a_added", "out_b_added", "mlp_evacuated"))
        s_vt, s_ct = sem("vec_transposed"), sem("c_act_ready")
        s_xtp, s_xt, s_ssq, s_sd = sem("x_transposed"), sem("xt_ready"), sem("x_squares"), sem("x_sd")
        s_diag, s_hnp = sem("diag_ready"), sem("x_scaled_transposed")
        s_acc, s_adat, s_adar, s_ada = (sem("ada_partial_done"), sem("ada_turned"), sem("ada_banks_read"), sem("ada_ready"))
        s_hn, s_v1, s_hi1, s_act1, s_act1p = (sem("x_over_rms"), sem("modulated"), sem("modulated_hi"),
                                              sem("modulated_lo_by_vector"), sem("modulated_lo_by_pool"))
        s_dve = sem("vector_step")
        s_sqb, s_qss, s_sdq, s_riq, s_qn = (sem("qk_squares"), sem("qk_sums"), sem("qk_sd"), sem("qk_rms_inverse"),
                                            sem("qk_normed"))
        s_gate = sem("ret_gate_ready")
        s_vtr, s_vn = sem("v_transposed"), sem("v_natural")
        s_sc, s_add, s_nm, s_exp, s_pn = (sem("scores_done"), sem("scores_biased"), sem("neg_max_ready"),
                                          sem("exp_done"), sem("probs_ready"))
        s_pt, s_pe, s_pv, s_ao = (sem("probs_transposed"), sem("probs_t_ready"), sem("attention_done"),
                                  sem("attention_stored"))
        s_ahi, s_amix = sem("attention_hi"), sem("attention_split")
        s_rt, s_rvn, s_kdn = sem("ret_kv_transposed"), sem("ret_v_natural"), sem("ret_k_natural")
        s_in, s_inn, s_qd = sem("inner_done"), sem("inner_decayed"), sem("q_decayed")
        s_o, s_kv, s_st = sem("ret_out_done"), sem("ret_kv_done"), sem("state_ready")
        s_var, s_rsd, s_nmr, s_on = sem("ret_var"), sem("ret_sd"), sem("ret_norm_terms"), sem("ret_normed")
        s_ot, s_rvl, s_rhi, s_rmix = sem("ret_transposed"), sem("ret_gated"), sem("ret_hi"), sem("ret_split")
        s_sq2, s_sqa, s_ss2, s_sd2 = sem("x1_squares"), sem("x1_squares_summed"), sem("x1_sums"), sem("x1_sd")
        s_h2, s_hi2, s_act2 = sem("normed2"), sem("normed2_hi"), sem("normed2_split")
        s_rsq, s_hih, s_hid = sem("relu_squared"), sem("hidden_hi"), sem("hidden_ready")
        s_ftr, s_ost = sem("final_transposed"), sem("out_staged")

        block = ctx.enter_context(nc.Block())

        def wait(eng, s, v):
            if not isinstance(v, int) or v > 0:
                eng.wait_ge(s, v)

        def wait_used(eng, t, mlp=False):
            if mlp or (isinstance(t, int) and t >= T_M):
                eng.wait_ge(s_mmm, t - (T_M - 1))
            elif t >= T_B:
                eng.wait_ge(s_mmb, t - T_B + 1)
            elif t >= T_A:
                eng.wait_ge(s_mma, 2 * (t - T_A + 1))
            elif t >= 0:
                eng.wait_ge(s_mmp, t + 1)

        def n_loads(t):
            return 2 if TQ <= t < TQ + GQA or T_A <= t < T_B else 1

        def loaded(t):
            return 16 * sum(n_loads(v) for v in range(t % 2, t + 1, 2))

        def k_tiles(t):
            return HK if isinstance(t, int) and T_A <= t < T_M else KT

        def pairs(eng, t0, n, step):
            assert t0 >= T_M and t0 + 2 * n < N_TILES
            with eng.Fori(0, n) as i:
                for s in range(2):
                    step(i * 2 + (t0 + s), s, i * 16 + loaded(t0 + s + 1))

        ACC1 = KT + 1

        NU = NB * NKV
        T_ATT = TQ + GQA
        ADA_OPS = 2
        ADA_TURN = {KT * (j + 1) // ADA_OPS + 1: j for j in range(4)}
        assert max(ADA_TURN) < RG and NU == N_PROJ - T_ATT

        NORM2_UNITS = {N_OUT + 2: 1, N_OUT + 3: 2, N_OUT + 4: 1, N_OUT + 5: 1, N_OUT + 6: 1, N_OUT + 7: 2}
        assert sum(NORM2_UNITS.values()) == KT

        @block.sync
        def _(sp):
            sp.dma_start(vrow[V_C:V_C + KT, :], c.rearrange("b (t p) -> (b t) p", p=P)).then_inc(s_c, 16)
            sp.dma_start(cst[:, 0:C_ONE], consts[:, 0:C_ONE]).then_inc(s_id, 16)
            for k in range(KT):
                for n in range(2 * k, min(2 * k + 2, NB)):
                    if n >= XS:
                        sp.wait_ge(s_hnp, n - XS + 1)
                        sp.wait_ge(s_xtp, n - XS + 1)
                        sp.wait_ge(s_ssq, n - XS + 1)
                    sp.dma_start(xin[:, n % XS, :], x[0, n * P:(n + 1) * P, :]).then_inc(s_xin[n], 16)
                sp.dma_start(wada1[k][:, :], w_ada[0, k * P:(k + 1) * P, 0:2 * D]).then_inc(s_wada1[k], 16)

            w_in_k = w_in[0].rearrange("(k p) n -> p k n", p=P)
            w_in_q = w_in[0][:, 0:NQ * HEAD].rearrange("(k p) (g n) -> p k g n", p=P, g=NKV)
            w_out_q = w_out[0][0:NQ * HEAD, :].rearrange("(g k d) n -> g d k n", g=NKV, k=GQA)
            w_out_r = w_out[0][NQ * HEAD:, :].rearrange("(k p) n -> p k n", p=P)
            w1_k = w_mlp1[0].rearrange("(k p) n -> p k n", p=P)
            w2_k = w_mlp2[0].rearrange("(q k p) n -> p q k n", p=P, q=QUARTERS)

            def load(slot, src, ks=KT):
                sp.dma_start(w_raw[:, slot, 0:ks, :], src).then_inc(s_raw[slot], 16)

            for t in range(T_M):
                wait(sp, s_wlo, t - 1)
                if TQ <= t < TQ + GQA:
                    for g in range(NKV):
                        col = (t - TQ) * HEAD
                        sp.dma_start(w_raw[:, t % 2, :, g * HEAD:(g + 1) * HEAD],
                                     w_in_q[:, :, g, col:col + HEAD]).then_inc(s_raw[t % 2], 16)
                elif t < N_PROJ:
                    col = t * P if t >= RQ else NQ * HEAD + t * P
                    load(t % 2, w_in_k[:, :, col:col + P])
                elif t < T_B:
                    for g in range(NKV):
                        sp.dma_start(w_raw[g * HEAD:(g + 1) * HEAD, t % 2, 0:HK, :],
                                     w_out_q[g][:, :, tokens(t - T_A)]).then_inc(s_raw[t % 2], 16)
                else:
                    load(t % 2, w_out_r[:, :, tokens((t - T_B) % N_OUT)], HK)
                if t == 1:
                    sp.dma_start(cst[:, C_ONE:], consts[:, C_ONE:]).then_inc(s_cst, 16)
            for q in range(QUARTERS):
                for first, src in ((T_M + q * 2 * KT, w1_k[:, :, q * D:(q + 1) * D]),
                                   (T_M + (q * 2 + 1) * KT, w2_k[:, q, :, :])):
                    with sp.Fori(0, KT // 2) as i:
                        for s in range(2):
                            sp.wait_ge(s_wlo, i * 2 + (first + s - 1))
                            load(s, src[:, :, bass.ds(i * 2 * P + s * P, P)])

        @block.gpsimd
        def _(pool):
            pool.dma_start(vrow[V_BADA:V_BADA + 48, :], b_ada.rearrange("l (t p) -> (l t) p", p=P)).then_inc(s_vrow, 16)
            pool.dma_start(vrow[V_N1:V_N1 + KT, :], norm1_g.rearrange("l (t p) -> (l t) p", p=P)).then_inc(s_vrow, 16)
            pool.dma_start(vrow[V_N2:V_N2 + KT, :], norm2_g.rearrange("l (t p) -> (l t) p", p=P)).then_inc(s_vrow, 16)
            pool.dma_start(vrow[V_RET:V_RET + RH, :], ret_norm_g.rearrange("l (t p) -> (l t) p", p=P)).then_inc(s_vrow, 16)
            for row, g in ((V_QG, q_norm_g), (V_KG, k_norm_g)):
                for half in range(2):
                    pool.dma_start(vrow[row:row + 1, half * HEAD:(half + 1) * HEAD], g).then_inc(s_vrow, 16)
            pool.dma_start(sink[:, :], sinks[0].partition_broadcast(P)).then_inc(s_sink, 16)

            for u in range(3, 2 * KT, 4):
                half, k = divmod(u, KT)
                cols = HALVES[half]
                pool.wait_ge(s_hi1, u + 1)
                pool.tensor_tensor(act_lo[:, k, cols], hn[:, k, cols], act_hi[:, k, cols].bitcast(F32),
                                   ALU.subtract).then_inc(s_act1p, 1)
            def load_ada2(u):
                j, k = divmod(u, KT)
                if u >= 2:
                    pool.wait_ge(s_acc, ACC1 + u - 1)
                pool.dma_start(wada2[:, u % 2, :],
                               w_ada[0, k * P:(k + 1) * P, (2 + j) * D:(3 + j) * D]).then_inc(s_wada2[u % 2], 16)

            pool.wait_ge(s_hnp, NB)
            pool.wait_ge(s_ssq, NB)
            load_ada2(0)
            load_ada2(1)
            pool.wait_ge(s_xt, NB)
            pool.dma_start(x_spill.rearrange("k p s -> p k s"), xt[:, :, :]).then_inc(s_spill, 16)
            for u in range(2, 4 * KT):
                load_ada2(u)

            def back(m):
                pool.dma_start(x1t[:, m, :], x_spill[m]).then_inc(s_back[m], 16)

            pool.wait_ge(s_spill, 16)
            pool.wait_ge(s_acc, ACC1 + 4 * KT)
            back(0)
            back(1)
            pool.wait_ge(s_vtr, 1)
            back(3)
            pool.wait_ge(s_sc, NU)
            back(2)

            def q_decayed(n):
                wait(pool, s_o, n)
                pool.tensor_tensor(qd[:, :, :], proj[:, RQ:RQ + RH, tokens(n)],
                                   cst[:, C_QDEC:C_QDEC + RH * P].rearrange("p (h n) -> p h n", h=RH),
                                   ALU.mult).then_inc(s_qd, 1)

            pool.wait_ge(s_evp, RQ + RH)
            pool.wait_ge(s_pt, NU)
            q_decayed(0)
            for m in range(4, KT):
                pool.wait_ge(s_amix, HK + m - 3)
                back(m)
            for n in range(1, NB):
                q_decayed(n)
            for half in range(2):
                for m in range(KT):
                    u = half * KT + m
                    pool.wait_ge(s_sq2, u + 1)
                    if m:
                        pool.wait_ge(s_sqa, u)
                        pool.tensor_tensor(sqa[:, half, :], sqa[:, half, :], sq2[:, u % 2, :], ALU.add).then_inc(s_sqa, 1)
                    else:
                        pool.tensor_copy(sqa[:, half, :], sq2[:, u % 2, :]).then_inc(s_sqa, 1)
            out_t = out[0].rearrange("(b p) n -> p b n", p=P)
            with pool.Fori(0, KT) as m:
                pool.wait_ge(s_ost, m + 1)
                pool.dma_start(out_t[:, :, bass.ds(m * P, P)], ost[:, :, :]).then_inc(s_out, 16)
            pool.wait_ge(s_out, 16 * KT)

        @block.tensor
        def _(pe):
            def chain(bank, slot, hi, lo, cols, ks, koff=0, before=None):
                for k in range(ks):
                    if before is not None:
                        before(k)
                    pe.matmul(bank, w_hi[:, slot, k, :], hi[:, koff + k, cols], start=(k == 0), stop=False)
                    pe.matmul(bank, w_hi[:, slot, k, :], lo[:, koff + k, cols], start=False, stop=False)
                    mm = pe.matmul(bank, w_lo[:, slot, k, :], hi[:, koff + k, cols], start=False, stop=(k == ks - 1))
                return mm

            pe.wait_ge(s_c, 16)
            pe.wait_ge(s_id, 16)
            pe.transpose(ps[:, 6, 0:KT], vrow[V_C:V_C + KT, :], cst[0:KT, C_ID:C_ID + KT]).then_inc(s_vt, 1)
            for n in range(NB + 1):
                if n < NB:
                    pe.wait_ge(s_xin[n], 16)
                    wait(pe, s_xt, n - 1)
                    for k in range(KT):
                        tr = pe.transpose(ps[:, 2 * (n % 2) + k // 4, tokens(k % 4)], xin[:, n % XS, tokens(k)], ident)
                    tr.then_inc(s_xtp, 1)
                if n:
                    pe.wait_ge(s_diag, n)
                    wait(pe, s_hn, n - 2)
                    if n == 2:
                        pe.wait_ge(s_ct, 1)
                    for k in range(KT):
                        mm = pe.matmul(ps[:, 4 + 2 * ((n - 1) % 2) + k // 4, tokens(k % 4)],
                                       xin[:, (n - 1) % XS, tokens(k)], diag[:, n - 1, :], start=True, stop=True)
                    mm.then_inc(s_hnp, 1)
            pe.wait_ge(s_vrow, 16 * 8)
            pe.wait_ge(s_hn, NB)
            pe.transpose(ps[:, 7, 0:V_ROWS], vrow[0:V_ROWS, :], cst[0:V_ROWS, C_ID:C_ID + V_ROWS]).then_inc(s_vt, 1)

            def ada_turn(j, bank):
                for m in range(KT):
                    tr = pe.transpose(ps[:, bank + m // 4, tokens(m % 4)],
                                      acc[:, j * D + m * P:j * D + (m + 1) * P], ident)
                tr.then_inc(s_adat, 1)

            pe.wait_ge(s_xt, NB)
            for i, j in enumerate((1, 0)):
                pe.wait_ge(s_acc, KT + i)
                ada_turn(j, 2 * j)

            def qk_sums(tile):
                i = 0 if tile == TK else tile - TQ + 1
                for half in range(2):
                    u = 2 * i + half
                    pe.wait_ge(s_sqb, u + 1)
                    wait(pe, s_sdq, u - 1)
                    pe.matmul(ps[:, 4 + half, :], blk, sqb[:, half, :], start=True, stop=True).then_inc(s_qss, 1)

            def turn_v():
                pe.wait_ge(s_evp, TV + 1)
                for n in range(NB):
                    tr = pe.transpose(ps[:, 6 + n // 4, (n % 4) * P:(n % 4 + 1) * P], proj[:, TV, tokens(n)], ident)
                tr.then_inc(s_vtr, 1)

            def scores(u):
                n, g = divmod(u, NKV)
                rows = slice(g * HEAD, (g + 1) * HEAD)
                lo = 0 if n else P
                if u == 0:
                    pe.wait_ge(s_qn, 10)
                wait(pe, s_add, u)
                for p in range(GQA):
                    mm = pe.matmul(ps[:, 4 + p // 2, (p % 2) * 256 + lo:(p % 2) * 256 + 256],
                                   proj[rows, TQ + p, tokens(n)],
                                   proj[rows, TK, (n - 1) * P + lo:(n + 1) * P], start=True, stop=True)
                mm.then_inc(s_sc, 1)

            def probs_turn(u):
                blocks = (0, 1) if u >= NKV else (1,)
                pe.wait_ge(s_pn, u + 1)
                wait(pe, s_ao, u)
                pe.wait_ge(s_adar, 2 + sum(T_ATT + u + 1 >= t for t in ADA_TURN))
                for b in blocks:
                    for p in range(GQA):
                        tr = pe.transpose(ps[:, 6 + b, tokens(p)], pr[u % 2][:, p, b * P:(b + 1) * P], ident)
                tr.then_inc(s_pt, 1)

            def attend(u):
                n, g = divmod(u, NKV)
                pe.wait_ge(s_pe, u + 1)
                if u == 0:
                    pe.wait_ge(s_vn, 1)
                for b in ((0, 1) if n else (1,)):
                    mm = pe.matmul(ps[g * HEAD:(g + 1) * HEAD, 6, :], vnat[:, n - 1 + b, g * HEAD:(g + 1) * HEAD],
                                   prt[:, b, :], start=(b == 0 or n == 0), stop=(b == 1))
                mm.then_inc(s_pv, 1)

            for half in range(2):
                for t in range(2):
                    def before(k):
                        if t == 0:
                            un = half * KT + k
                            if un % 4 == 3:
                                pe.wait_ge(s_act1p, un // 4 + 1)
                            else:
                                pe.wait_ge(s_act1, un - un // 4 + 1)
                        if (half, t, k) == (1, 1, 7):
                            pe.wait_ge(s_cst, 16)
                            qk_sums(TK)
                    if half == 0:
                        pe.wait_ge(s_wlo, t + 1)
                        pe.wait_ge(s_adar, 2)
                    mm = chain(ps[:, 2 * t + half, :], t, act_hi, act_lo, HALVES[half], KT, 0, before)
                    if half == 1:
                        mm.then_inc(s_mmp, 1)
            for t in range(2, N_PROJ):
                slot, u = t % 2, t - T_ATT
                pe.wait_ge(s_wlo, t + 1)
                pe.wait_ge(s_evp, t - 1)
                for half in range(2):
                    def before(k):
                        if (half, k) == (0, 5) and t <= T_ATT and t - 1 != TV:
                            qk_sums(t - 1)
                        if (half, k) == (0, 5) and t == TV + 2:
                            turn_v()
                        if (half, k) == (0, 4) and t in ADA_TURN:
                            j = ADA_TURN[t]
                            pe.wait_ge(s_acc, ACC1 + KT * (j + 1))
                            pe.wait_ge(s_vn, 1)
                            wait(pe, s_ao, u - 1)
                            ada_turn(j, 6)
                        if (half, k) == (1, 4) and u >= 1:
                            probs_turn(u - 1)
                    mm = chain(ps[:, 2 * slot + half, :], slot, act_hi, act_lo, HALVES[half], KT, 0, before)
                mm.then_inc(s_mmp, 1)
                if u >= 1:
                    attend(u - 1)
                if u >= 0:
                    scores(u)

            def ret_in(n):
                wait(pe, s_kdn, n)
                wait(pe, s_rvn, n)
                for h in range(RH):
                    pe.transpose(ps[:, 2, tokens(h)], proj[:, RK + h, tokens(n)], ident)
                for h in range(RH):
                    tr = pe.transpose(ps[:, 3, tokens(h)], proj[:, RV + h, tokens(n)], ident)
                tr.then_inc(s_rt, 1)
                wait(pe, s_inn, n)
                if n == 0:
                    pe.wait_ge(s_add, NU)
                for h in range(RH):
                    mm = pe.matmul(ps[:, 4, tokens(h)], proj[:, RK + h, tokens(n)], proj[:, RQ + h, tokens(n)],
                                   start=True, stop=True)
                mm.then_inc(s_in, 1)

            def ret_out(n):
                pe.wait_ge(s_kdn, n + 1)
                pe.wait_ge(s_rvn, n + 1)
                wait(pe, s_st, n)
                if n + 1 < NB:
                    for h in range(RH):
                        mm = pe.matmul(ps[:, 6, tokens(h)], kdn[:, h, :], rvn[:, h, :], start=True, stop=True)
                    mm.then_inc(s_kv, 1)
                pe.wait_ge(s_inn, n + 1)
                pe.wait_ge(s_qd, n + 1)
                wait(pe, s_on, n)
                for h in range(RH):
                    bank = ps[:, 5, tokens(h)]
                    mm = pe.matmul(bank, inn[:, h, :], rvn[:, h, :], start=True, stop=(n == 0))
                    if n:
                        mm = pe.matmul(bank, qd[:, h, :], st[n % 2][:, h, :], start=False, stop=True)
                mm.then_inc(s_o, 1)

            def ret_turn(n):
                pe.wait_ge(s_on, n + 1)
                wait(pe, s_rvl, n)
                for h in range(RH):
                    tr = pe.transpose(ps[:, 7, tokens(h)], onr[:, h, :], ident)
                tr.then_inc(s_ot, 1)

            for m in range(N_OUT):
                t = T_A + m
                pe.wait_ge(s_wlo, t + 1)
                for half in range(2):
                    def before(k):
                        if m == 0:
                            pe.wait_ge(s_amix, half * HK + k + 1)
                    if m == 0:
                        pe.wait_ge(s_evp, N_PROJ - 1)
                    wait(pe, s_eva, 2 * m + half - 1)
                    chain(ps[:, half, :], t % 2, act_hi, act_lo, HALVES[half], HK, 0, before).then_inc(s_mma, 1)
                    if half == 0 and m == 0:
                        pe.wait_ge(s_evp, N_PROJ)
                        ret_in(0)
                        probs_turn(NU - 1)
                        attend(NU - 1)
                    elif half == 0:
                        if m >= 2:
                            ret_turn(m - 2)
                        ret_out(m - 1)
                        ret_in(m)

            def x1_sums(half):
                pe.wait_ge(s_sqa, (half + 1) * KT)
                wait(pe, s_sd2, half)
                pe.matmul(ps[:, 4, :], ones, sqa[:, half, :], start=True, stop=True).then_inc(s_ss2, 1)

            for b in range(2 * N_OUT):
                t, half = T_B + b, b // N_OUT
                pe.wait_ge(s_wlo, t + 1)
                if b < 2:
                    pe.wait_ge(s_eva, 2 * N_OUT - 1 + b)
                wait(pe, s_evb, b - 1)
                if b == 0:
                    pe.wait_ge(s_rmix, NB // 2)
                if b == N_OUT:
                    pe.wait_ge(s_rmix, NB)
                chain(ps[:, b % 2, :], t % 2, act_hi, act_lo, HALVES[half], HK, HK).then_inc(s_mmb, 1)
                if b == 0:
                    ret_turn(NB - 2)
                    ret_out(NB - 1)
                if b == 3:
                    ret_turn(NB - 1)
                if b == N_OUT + 1:
                    x1_sums(0)

            def product(t, slot, hi, lo, before=None):
                pe.wait_ge(s_wlo, t + 1)
                pe.wait_ge(s_evm, t - (T_M + 1))
                for half in range(2):
                    mm = chain(ps[:, 2 * slot + half, :], slot, hi, lo, HALVES[half], KT, 0,
                               (lambda k: before(half, k)) if before else None)
                mm.then_inc(s_mmm, 1)

            for half in range(2):
                for s in range(2):
                    def before(k):
                        if s == 0:
                            pe.wait_ge(s_act2, half * KT + k + 1)
                        if (half, s, k) == (0, 0, 5):
                            x1_sums(1)
                    if half == 0:
                        pe.wait_ge(s_wlo, T_M + s + 1)
                        if s == 0:
                            pe.wait_ge(s_evb, 2 * N_OUT)
                    mm = chain(ps[:, 2 * s + half, :], s, act_hi, act_lo, HALVES[half], KT, 0, before)
                    if half == 1:
                        mm.then_inc(s_mmm, 1)
            for q in range(QUARTERS):
                t0 = T_M + q * 2 * KT
                with pe.Fori(1 if q == 0 else 0, KT // 2) as i:
                    for s in range(2):
                        product(i * 2 + (t0 + s), s, act_hi, act_lo)
                t1 = t0 + KT
                product(t1, 0, hid_hi, hid_lo, lambda half, k: pe.wait_ge(s_hid, q * KT + k + 1) if half == 0 else None)
                product(t1 + 1, 1, hid_hi, hid_lo)
                if q < QUARTERS - 1:
                    with pe.Fori(1, KT // 2) as i:
                        for s in range(2):
                            product(i * 2 + (t1 + s), s, hid_hi, hid_lo)

            def turn(m):
                pe.wait_ge(s_evm, m + (N_TILES - KT - T_M + 1))
                wait(pe, s_ost, m)
                for n in range(NB):
                    tr = pe.transpose(ps[:, 4 + n // 4, tokens(n % 4)], fin[:, tokens(n)], ident)
                tr.then_inc(s_ftr, 1)

            turn(0)
            with pe.Fori(1, KT // 2) as i:
                for s in range(2):
                    product(i * 2 + (t1 + s), s, hid_hi, hid_lo)
                    turn(i * 2 + (s - 1))
            turn(KT - 1)

        @block.scalar
        def _(act):
            def split_hi(t, slot, count, mlp=False):
                ks = k_tiles(t)
                act.wait_ge(s_raw[slot], count)
                wait_used(act, t - 2, mlp)
                act.activation(w_hi[:, slot, 0:ks, :], w_raw[:, slot, 0:ks, :], ACT.Copy).then_inc(s_whi, 1)

            def split_next(t):
                split_hi(t + 1, (t + 1) % 2, loaded(t + 1))

            act.wait_ge(s_vt, 1)
            act.activation(ct[:, :], ps[:, 6, 0:KT], ACT.Silu).then_inc(s_ct, 1)
            act.wait_ge(s_dve, 1)
            for n in range(NB + 1):
                if n < NB:
                    act.wait_ge(s_xin[n], 16)
                    wait(act, s_ssq, n - 1)
                    act.activation(sqj[:, n % 2, :], xin[:, n % XS, :], ACT.Square,
                                   accum_out=ss[:, n:n + 1]).then_inc(s_ssq, 1)
                    act.wait_ge(s_ssq, n + 1)
                    act.activation(sd8[:, n:n + 1], ss[:, n:n + 1], ACT.Sqrt, bias=eps[:, :], scale=1.0 / D).then_inc(s_sd, 1)
                    act.wait_ge(s_xtp, n + 1)
                    act.activation(xt[:, :, tokens(n)], bank_pair(n % 2).rearrange("p (k n) -> p k n", k=KT),
                                   ACT.Copy).then_inc(s_xt, 1)
                if n:
                    act.wait_ge(s_hnp, n)
                    act.activation(hn[:, :, tokens(n - 1)],
                                   bank_pair(2 + (n - 1) % 2).rearrange("p (k n) -> p k n", k=KT), ACT.Copy).then_inc(s_hn, 1)
            split_next(-1)
            for u in range(2 * KT):
                half, k = divmod(u, KT)
                act.wait_ge(s_v1, u + 1)
                act.activation(act_hi[:, k, HALVES[half]], hn[:, k, HALVES[half]], ACT.Copy).then_inc(s_hi1, 1)
                if u == 3:
                    split_next(0)

            def qk_sd(tile):
                i = 0 if tile == TK else tile - TQ + 1
                for half in range(2):
                    u = 2 * i + half
                    act.wait_ge(s_qss, u + 1)
                    wait(act, s_riq, u - 1)
                    act.activation(sdq[:, half, :], ps[:, 4 + half, :], ACT.Sqrt, bias=eps[:, :],
                                   scale=1.0 / HEAD).then_inc(s_sdq, 1)

            def exps(u):
                i, lo = u % 2, 0 if u >= NKV else P
                act.wait_ge(s_nm, u + 1)
                for p in range(GQA):
                    act.activation(pr[i][:, p, lo:], pr[i][:, p, lo:], ACT.Exp, bias=nm[:, i, p:p + 1],
                                   accum_out=den[:, i, p:p + 1])
                act.activation(ex[:, i, :], es[:, i, :], ACT.Exp).then_inc(s_exp, 1)

            def probs_copy(u):
                b0 = 0 if u >= NKV else 1
                act.wait_ge(s_pt, u + 1)
                wait(act, s_pv, u)
                act.activation(prt[:, b0:, :], ps[:, 6 + b0:8, :], ACT.Copy).then_inc(s_pe, 1)

            def attn_store(u):
                n, g = divmod(u, NKV)
                rows = slice(g * HEAD, (g + 1) * HEAD)
                act.wait_ge(s_pv, u + 1)
                act.activation(proj[rows, TQ:TQ + GQA, tokens(n)], ps[rows, 6, :].rearrange("p (k n) -> p k n", k=GQA),
                               ACT.Copy).then_inc(s_ao, 1)

            def attn_hi(half):
                for k in range(HK):
                    act.wait_ge(s_ao, (half + 1) * NU // 2)
                    act.activation(act_hi[:, k, HALVES[half]], proj[:, TQ + k, HALVES[half]], ACT.Copy).then_inc(s_ahi, 1)

            for t in range(N_PROJ):
                u = t - T_ATT
                if u >= 1:
                    exps(u - 1)
                if t:
                    split_next(t)
                if 0 < t <= T_ATT and t - 1 != TV:
                    qk_sd(t - 1)
                if t == TV + 2:
                    act.wait_ge(s_vtr, 1)
                    act.activation(flat(vnat[:, :, :]), flat(ps[:, 6:8, :]), ACT.Copy).then_inc(s_vn, 1)
                if u >= 1:
                    probs_copy(u - 1)
                if t == 9:
                    act.wait_ge(s_spill, 16)
                if t == RG:
                    act.wait_ge(s_adat, 6)
                act.wait_ge(s_mmp, t + 1)
                if t == N_PROJ - 1:
                    attn_hi(0)
                act.activation(proj[:, t, :], bank_pair(t % 2), ACT.Silu if t >= RG else ACT.Copy).then_inc(s_evp, 1)
                if t < T_ATT and t != TV:
                    i = 0 if t == TK else t - TQ + 1
                    wait(act, s_qss, 2 * i)
                    act.wait_ge(s_evp, t + 1)
                    for half in range(2):
                        act.activation(sqb[:, half, :], proj[:, t, HALVES[half]], ACT.Square).then_inc(s_sqb, 1)
                if u >= 1:
                    attn_store(u - 1)

            exps(NU - 1)
            split_next(T_A)

            def ret_v(n):
                act.wait_ge(s_rt, n + 1)
                wait(act, s_o, n)
                act.activation(flat(rvn[:, :, :]), ps[:, 3, :], ACT.Copy).then_inc(s_rvn, 1)

            def ret_hi(n):
                act.wait_ge(s_rvl, n + 1)
                act.activation(act_hi[:, HK:, tokens(n)], rvl[:, :, :], ACT.Copy).then_inc(s_rhi, 1)

            def ret_norm(n):
                act.wait_ge(s_var, n + 1)
                act.activation(rsd[:, :], mv[:, :, 1], ACT.Sqrt, bias=eps[:, :]).then_inc(s_rsd, 1)
                act.wait_ge(s_nmr, n + 1)
                wait(act, s_ot, n)
                for h in range(RH):
                    on = act.activation(onr[:, h, :], ps[:, 5, tokens(h)], ACT.Identity,
                                        bias=nmr[:, h:h + 1], scale=rri[:, h:h + 1])
                on.then_inc(s_on, 1)

            ret_v(0)
            probs_copy(NU - 1)
            attn_store(NU - 1)
            attn_hi(1)
            for m in range(1, N_OUT):
                split_next(T_A + m)
                if m >= 2:
                    ret_hi(m - 2)
                ret_v(m)
                ret_norm(m - 1)

            unit = [0]

            def norm2_sd(half):
                act.wait_ge(s_ss2, half + 1)
                act.activation(sd2[:, half, :], ps[:, 4, :], ACT.Sqrt, bias=eps[:, :], scale=1.0 / D).then_inc(s_sd2, 1)

            def norm2_hi():
                half, k = divmod(unit[0], KT)
                act.wait_ge(s_h2, unit[0] + 1)
                act.activation(act_hi[:, k, HALVES[half]], ht2[:, unit[0] % 2, :], ACT.Identity,
                               bias=ada[:, 3 * KT + k:3 * KT + k + 1]).then_inc(s_hi2, 1)
                unit[0] += 1

            for b in range(2 * N_OUT):
                half, m = divmod(b, N_OUT)
                split_next(T_B + b)
                if b == 0:
                    ret_hi(NB - 2)
                    ret_norm(NB - 1)
                if b == 3:
                    ret_hi(NB - 1)
                act.wait_ge(s_evb, b + 1)
                wait(act, s_sqa, b - 1)
                act.activation(sq2[:, b % 2, :], x1t[:, m, HALVES[half]], ACT.Square).then_inc(s_sq2, 1)
                if b == N_OUT + 1:
                    norm2_sd(0)
                for _ in range(NORM2_UNITS.get(b, 0)):
                    norm2_hi()
            split_next(T_M)
            norm2_sd(1)
            for _ in range(KT):
                norm2_hi()

            def up(q):
                t0 = T_M + q * 2 * KT

                def step(t, slot, count):
                    split_hi(t + 1, 1 - slot, count, mlp=True)
                    relu_split(t, slot, t - t0, q)
                return step

            def relu_split(t, slot, m, q):
                act.wait_ge(s_mmm, t - (T_M - 1))
                wait(act, s_rsq, m + q * KT)
                act.activation(rel[:, :], bank_pair(slot), ACT.Relu).then_inc(s_evm, 1)
                act.wait_ge(s_rsq, m + (q * KT + 1))
                act.activation(tile_of(hid_hi, m), rsq[:, :], ACT.Copy).then_inc(s_hih, 1)

            def down(t, slot, count):
                split_hi(t + 1, 1 - slot, count, mlp=True)

            for q in range(QUARTERS):
                t0 = T_M + q * 2 * KT
                if q == 0:
                    relu_split(t0, 0, 0, 0)
                    up(0)(t0 + 1, 1, loaded(t0 + 2))
                    pairs(act, t0 + 2, KT // 2 - 1, up(0))
                else:
                    pairs(act, t0, KT // 2, up(q))
                if q < QUARTERS - 1:
                    pairs(act, t0 + KT, KT // 2, down)

            def stage(m):
                act.wait_ge(s_ftr, m + 1)
                wait(act, s_out, m * 16)
                act.activation(flat(ost[:, :, :]), flat(ps[:, 4:6, :]), ACT.Copy).then_inc(s_ost, 1)

            t1 = N_TILES - KT
            down(t1, 0, loaded(t1 + 1))
            down(t1 + 1, 1, loaded(t1 + 2))
            stage(0)

            def down_last(t, slot, count):
                down(t, slot, count)
                stage(t - (t1 + 1))

            pairs(act, t1 + 2, KT // 2 - 2, down_last)
            down_last(N_TILES - 2, 0, loaded(N_TILES - 1))
            stage(KT - 2)
            stage(KT - 1)

        @block.vector
        def _(dve):
            own = [0]

            def link(ins):
                own[0] += 1
                ins.then_inc(s_dve, 1)
                dve.wait_ge(s_dve, own[0])

            def split_lo(t, slot):
                ks = k_tiles(t)
                dve.wait_ge(s_whi, t + 1)
                dve.tensor_tensor(w_lo[:, slot, 0:ks, :], w_raw[:, slot, 0:ks, :], w_hi[:, slot, 0:ks, :].bitcast(F32),
                                  ALU.subtract).then_inc(s_wlo, 1)

            def split_next(t):
                split_lo(t + 1, (t + 1) % 2)

            link(dve.memset(eps[:, :], EPS))
            def ada_step(j, k, row, s_row, u):
                dve.wait_ge(s_row, u)
                if k == 0:
                    dve.tensor_scalar(j, row, ct[:, 0:1], None, ALU.mult).then_inc(s_acc, 1)
                else:
                    dve.scalar_tensor_tensor(out=j, in0=row, scalar=ct[:, k:k + 1], in1=j,
                                             op0=ALU.mult, op1=ALU.add).then_inc(s_acc, 1)

            def rms_diag(n):
                dve.wait_ge(s_sd, n + 1)
                link(dve.reciprocal(rs8[:, n:n + 1], sd8[:, n:n + 1]))
                dve.tensor_scalar(diag[:, n, :], ident, rs8[:, n:n + 1], None, ALU.mult).then_inc(s_diag, 1)

            dve.wait_ge(s_id, 16)
            dve.wait_ge(s_ct, 1)
            for k in range(KT):
                for n in range(2 * k, min(2 * k + 2, NB)):
                    rms_diag(n)
                wait(dve, s_acc, k)
                if k < KT - 1:
                    ada_step(acc[:, 0:2 * D], k, wada1[k][:, :], s_wada1[k], 16)
                else:
                    ada_step(acc[:, D:2 * D], k, wada1[k][:, D:2 * D], s_wada1[k], 16)
                    ada_step(acc[:, 0:D], k, wada1[k][:, 0:D], s_wada1[k], 16)
                if k == KT - 3:
                    dve.wait_ge(s_vt, 2)
                    link(dve.tensor_copy(vec[:, :], ps[:, 7, 0:V_ROWS]))
                    link(dve.tensor_scalar(qg8[:, :], vec[:, V_QG:V_QG + 1], HEAD ** -0.5, None, ALU.mult))
                    dve.wait_ge(s_sink, 16)
                    link(dve.tensor_scalar(nsink[:, :], sink[:, :], -1.0, None, ALU.mult))

            def ada_vector(j, bank, turned):
                dst = ada[:, j * KT:(j + 1) * KT]
                dve.wait_ge(s_adat, turned)
                dve.tensor_reduce(dst, ps[:, bank:bank + 2, :].rearrange("p b (m r) -> p (b m) r", r=P), AX_X,
                                  ALU.add).then_inc(s_adar, 1)
                dve.wait_ge(s_adar, turned)
                bias = vec[:, V_BADA + j * KT:V_BADA + (j + 1) * KT]
                if j in (1, 4):
                    gain, a = (V_N1, a1) if j == 1 else (V_N2, a2)
                    link(dve.scalar_tensor_tensor(out=dst, in0=dst, scalar=1.0, in1=bias, op0=ALU.add, op1=ALU.add))
                    link(dve.tensor_tensor(a[:, :], dst, vec[:, gain:gain + KT], ALU.mult))
                else:
                    link(dve.tensor_tensor(dst, dst, bias, ALU.add))

            ada_vector(1, 2, 1)
            ada_vector(0, 0, 2)

            def low1(u):
                half, k = divmod(u, KT)
                if u % 4 == 3:
                    return
                dve.wait_ge(s_hi1, u + 1)
                dve.tensor_tensor(act_lo[:, k, HALVES[half]], hn[:, k, HALVES[half]],
                                  act_hi[:, k, HALVES[half]].bitcast(F32), ALU.subtract).then_inc(s_act1, 1)

            dve.wait_ge(s_hn, NB)
            split_next(-1)
            for u in range(2 * KT):
                half, k = divmod(u, KT)
                dve.tensor_scalar(hn[:, k, HALVES[half]], hn[:, k, HALVES[half]], a1[:, k:k + 1], ada[:, k:k + 1],
                                  ALU.mult, ALU.add).then_inc(s_v1, 1)
                if u:
                    low1(u - 1)
                if u == KT:
                    split_next(0)
            low1(2 * KT - 1)

            def qk_norm(tile):
                i = 0 if tile == TK else tile - TQ + 1
                gain = vec[:, V_KG:V_KG + 1] if tile == TK else qg8[:, 0:1]
                for half in range(2):
                    u = 2 * i + half
                    dve.wait_ge(s_sdq, u + 1)
                    wait(dve, s_qn, u - 1)
                    dve.reciprocal(riq[:, half, :], sdq[:, half, :]).then_inc(s_riq, 1)
                    dve.wait_ge(s_riq, u + 1)
                    dve.scalar_tensor_tensor(out=proj[:, tile, HALVES[half]], in0=proj[:, tile, HALVES[half]], scalar=gain,
                                             in1=riq[:, half, :], op0=ALU.mult, op1=ALU.mult).then_inc(s_qn, 1)

            def bias_max(u):
                g, i, lo = u % NKV, u % 2, 0 if u >= NKV else P
                dve.wait_ge(s_sc, u + 1)
                wait(dve, s_pt, u - 1)
                for p in range(GQA):
                    ad = dve.scalar_tensor_tensor(
                        out=pr[i][:, p, lo:], in0=dist[:, lo:], scalar=-SLOPES[g * GQA + p],
                        in1=ps[:, 4 + p // 2, (p % 2) * 256 + lo:(p % 2) * 256 + 256], op0=ALU.mult, op1=ALU.add)
                ad.then_inc(s_add, 1)
                dve.wait_ge(s_add, u + 1)
                link(dve.tensor_reduce(mx[:, i, :], pr[i][:, :, lo:], AX_X, ALU.max))
                heads = slice(g * GQA, (g + 1) * GQA)
                link(dve.scalar_tensor_tensor(out=nm[:, i, :], in0=mx[:, i, :], scalar=-1.0, in1=nsink[:, heads],
                                              op0=ALU.mult, op1=ALU.min))
                dve.tensor_tensor(es[:, i, :], nm[:, i, :], sink[:, heads], ALU.add).then_inc(s_nm, 1)

            def normalise(u):
                i, lo = u % 2, 0 if u >= NKV else P
                dve.wait_ge(s_exp, u + 1)
                link(dve.tensor_tensor(den[:, i, :], den[:, i, :], ex[:, i, :], ALU.add))
                link(dve.reciprocal(rd[:, i, :], den[:, i, :]))
                for p in range(GQA):
                    pn = dve.tensor_scalar(pr[i][:, p, lo:], pr[i][:, p, lo:], rd[:, i, p:p + 1], None, ALU.mult)
                pn.then_inc(s_pn, 1)

            def attn_lo(half):
                for k in range(HK):
                    dve.wait_ge(s_ahi, half * HK + k + 1)
                    dve.tensor_tensor(act_lo[:, k, HALVES[half]], proj[:, TQ + k, HALVES[half]],
                                      act_hi[:, k, HALVES[half]].bitcast(F32), ALU.subtract).then_inc(s_amix, 1)

            def ada_step2(a):
                j, k = divmod(a, KT)
                dve.wait_ge(s_acc, ACC1 + a)
                ada_step(acc[:, j * D:(j + 1) * D], k, wada2[:, a % 2, :], s_wada2[a % 2], 16 * (a // 2 + 1))

            for t in range(N_PROJ):
                u = t - T_ATT
                a = ADA_OPS * (t - 1)
                if 0 <= a < 4 * KT:
                    ada_step2(a)
                if u >= 1:
                    normalise(u - 1)
                if t:
                    split_next(t)
                if 0 < t <= T_ATT and t - 1 != TV:
                    qk_norm(t - 1)
                if t in ADA_TURN:
                    j = 2 + ADA_TURN[t]
                    ada_vector(j, 6, j + 1)
                if 0 <= a < 4 * KT:
                    ada_step2(a + 1)
                if t == N_PROJ - 1:
                    attn_lo(0)
                if u >= 0:
                    bias_max(u)

            def ret_k(n):
                dve.wait_ge(s_rt, n + 1)
                wait(dve, s_o, n)
                kdec = cst[:, C_KDEC:C_KDEC + RH].unsqueeze(2).broadcast_to([P, RH, P])
                dve.tensor_tensor(kdn[:, :, :], ps[:, 2, :].rearrange("p (h n) -> p h n", h=RH), kdec,
                                  ALU.mult).then_inc(s_kdn, 1)

            def ret_inner(n):
                dve.wait_ge(s_in, n + 1)
                dve.tensor_tensor(flat(inn[:, :, :]), ps[:, 4, :], cst[:, C_DEC:C_DEC + RH * P],
                                  ALU.mult).then_inc(s_inn, 1)

            def ret_state(n):
                dve.wait_ge(s_kv, n + 1)
                wait(dve, s_o, n)
                new, old = st[(n + 1) % 2], st[n % 2]
                if n == 0:
                    dve.tensor_copy(flat(new[:, :, :]), ps[:, 6, :]).then_inc(s_st, 1)
                    return
                dve.wait_ge(s_st, n)
                for h in range(RH):
                    sn = dve.scalar_tensor_tensor(out=new[:, h, :], in0=old[:, h, :],
                                                  scalar=cst[:, C_CHUNK + h:C_CHUNK + h + 1],
                                                  in1=ps[:, 6, tokens(h)], op0=ALU.mult, op1=ALU.add)
                sn.then_inc(s_st, 1)

            def ret_stats(n):
                dve.wait_ge(s_o, n + 1)
                for h in range(RH):
                    b = dve.bn_stats(bn[:, h, :], ps[:, 5, tokens(h)])
                link(b)
                wait(dve, s_on, n)
                for h in range(RH):
                    b = dve.bn_aggr(mv[:, h, :], bn[:, h, :])
                b.then_inc(s_var, 1)

            def ret_terms(n):
                dve.wait_ge(s_rsd, n + 1)
                dve.wait_ge(s_var, n + 1)
                link(dve.reciprocal(rri[:, :], rsd[:, :]))
                dve.scalar_tensor_tensor(out=nmr[:, :], in0=mv[:, :, 0], scalar=-1.0, in1=rri[:, :],
                                         op0=ALU.mult, op1=ALU.mult).then_inc(s_nmr, 1)

            def ret_gate(n):
                dve.wait_ge(s_ot, n + 1)
                wait(dve, s_rmix, n)
                dve.tensor_tensor(rvl[:, :, :], ps[:, 7, :].rearrange("p (h n) -> p h n", h=RH),
                                  proj[:, RG:RG + RH, tokens(n)], ALU.mult).then_inc(s_rvl, 1)

            def ret_lo(n):
                dve.wait_ge(s_rhi, n + 1)
                dve.tensor_tensor(act_lo[:, HK:, tokens(n)], rvl[:, :, :], act_hi[:, HK:, tokens(n)].bitcast(F32),
                                  ALU.subtract).then_inc(s_rmix, 1)

            def add_a(m, half):
                if half == 0:
                    dve.wait_ge(s_back[m], 16)
                dve.wait_ge(s_mma, 2 * m + half + 1)
                dve.scalar_tensor_tensor(out=x1t[:, m, HALVES[half]], in0=ps[:, half, :],
                                         scalar=ada[:, 2 * KT + m:2 * KT + m + 1], in1=x1t[:, m, HALVES[half]],
                                         op0=ALU.mult, op1=ALU.add).then_inc(s_eva, 1)

            normalise(NU - 1)
            split_next(T_A)
            add_a(0, 0)
            ret_k(0)
            dve.wait_ge(s_pt, NU)
            ret_inner(0)
            attn_lo(1)
            dve.wait_ge(s_evp, N_PROJ)
            for h in range(RH):
                dve.tensor_scalar(proj[:, RG + h, :], proj[:, RG + h, :], vec[:, V_RET + h:V_RET + h + 1], None,
                                  ALU.mult).then_inc(s_gate, 1)
            add_a(0, 1)
            dve.wait_ge(s_gate, RH)
            for m in range(1, N_OUT):
                split_next(T_A + m)
                add_a(m, 0)
                if m >= 2:
                    ret_gate(m - 2)
                ret_state(m - 1)
                ret_stats(m - 1)
                if m >= 2:
                    ret_lo(m - 2)
                ret_k(m)
                ret_inner(m)
                ret_terms(m - 1)
                add_a(m, 1)

            unit = [0]

            def norm2_lo(u):
                half, k = divmod(u, KT)
                dve.wait_ge(s_hi2, u + 1)
                dve.scalar_tensor_tensor(out=act_lo[:, k, HALVES[half]], in0=ht2[:, u % 2, :],
                                         scalar=ada[:, 3 * KT + k:3 * KT + k + 1],
                                         in1=act_hi[:, k, HALVES[half]].bitcast(F32), op0=ALU.add,
                                         op1=ALU.subtract).then_inc(s_act2, 1)

            def norm2_unit():
                u = unit[0]
                half, k = divmod(u, KT)
                if k == 0:
                    dve.wait_ge(s_sd2, half + 1)
                    link(dve.reciprocal(rinv2[:, half, :], sd2[:, half, :]))
                wait(dve, s_act2, u - 1)
                dve.scalar_tensor_tensor(out=ht2[:, u % 2, :], in0=x1t[:, k, HALVES[half]], scalar=a2[:, k:k + 1],
                                         in1=rinv2[:, half, :], op0=ALU.mult, op1=ALU.mult).then_inc(s_h2, 1)
                if k:
                    norm2_lo(u - 1)
                unit[0] += 1

            for b in range(2 * N_OUT):
                half, m = divmod(b, N_OUT)
                split_next(T_B + b)
                if b == 0:
                    ret_gate(NB - 2)
                    ret_stats(NB - 1)
                    ret_lo(NB - 2)
                    ret_terms(NB - 1)
                dve.wait_ge(s_mmb, b + 1)
                dve.scalar_tensor_tensor(out=x1t[:, m, HALVES[half]], in0=ps[:, b % 2, :],
                                         scalar=ada[:, 2 * KT + m:2 * KT + m + 1], in1=x1t[:, m, HALVES[half]],
                                         op0=ALU.mult, op1=ALU.add).then_inc(s_evb, 1)
                if b == 3:
                    ret_gate(NB - 1)
                    ret_lo(NB - 1)
                for _ in range(NORM2_UNITS.get(b, 0)):
                    norm2_unit()
            norm2_lo(KT - 1)
            split_next(T_M)
            for _ in range(KT):
                norm2_unit()
            norm2_lo(2 * KT - 1)

            def square_split(t, m, q):
                dve.wait_ge(s_evm, t - (T_M - 1))
                wait(dve, s_hid, m + q * KT)
                dve.tensor_tensor(rsq[:, :], rel[:, :], rel[:, :], ALU.mult).then_inc(s_rsq, 1)
                dve.wait_ge(s_hih, m + (q * KT + 1))
                dve.tensor_tensor(tile_of(hid_lo, m), rsq[:, :], tile_of(hid_hi, m).bitcast(F32),
                                  ALU.subtract).then_inc(s_hid, 1)

            def up(q):
                t0 = T_M + q * 2 * KT

                def step(t, slot, count):
                    split_lo(t + 1, 1 - slot)
                    square_split(t, t - t0, q)
                return step

            def down(q):
                t1 = T_M + (q * 2 + 1) * KT

                def step(t, slot, count):
                    if not isinstance(t, int) or t + 1 < N_TILES:
                        split_lo(t + 1, 1 - slot)
                    m = t - t1
                    dve.wait_ge(s_mmm, t - (T_M - 1))
                    if q == QUARTERS - 1:
                        wait(dve, s_ftr, m)
                    dve.scalar_tensor_tensor(out=tile_of(x1t, m) if q < QUARTERS - 1 else fin[:, :], in0=bank_pair(slot),
                                             scalar=ada[:, bass.ds(m + 5 * KT, 1)], in1=tile_of(x1t, m),
                                             op0=ALU.mult, op1=ALU.add).then_inc(s_evm, 1)
                return step

            for q in range(QUARTERS):
                t0 = T_M + q * 2 * KT
                if q == 0:
                    square_split(t0, 0, 0)
                    up(0)(t0 + 1, 1, 0)
                    pairs(dve, t0 + 2, KT // 2 - 1, up(0))
                else:
                    pairs(dve, t0, KT // 2, up(q))
                if q < QUARTERS - 1:
                    pairs(dve, t0 + KT, KT // 2, down(q))
            t1 = N_TILES - KT
            for s in range(2):
                down(QUARTERS - 1)(t1 + s, s, 0)
            pairs(dve, t1 + 2, KT // 2 - 2, down(QUARTERS - 1))
            for s in range(2):
                down(QUARTERS - 1)(N_TILES - 2 + s, s, 0)


_INS = ["x", "c", "norm1_g", "norm2_g", "w_ada", "b_ada", "w_in", "q_norm_g", "k_norm_g", "sinks", "ret_norm_g",
        "w_out", "w_mlp1", "w_mlp2"]


def kernel(**inputs):
    import numpy as np
    import concourse.bacc as bacc
    from concourse.bass_utils import run_bass_kernel_spmd as run

    nc = bacc.Bacc("TRN2", target_bir_lowering=False, num_devices=1)
    arrays, args = {}, []
    for name in _INS:
        a = np.ascontiguousarray(inputs[name])
        arrays[f"in_{name}_dram"] = a
        args.append(nc.dram_tensor(f"in_{name}_dram", a.shape, mybir.dt.from_np(a.dtype), kind="ExternalInput").ap())
    arrays["shape_constants"] = shape_constants()
    args.append(nc.dram_tensor("shape_constants", (P, C_W), F32, kind="ExternalInput").ap())
    args.append(nc.dram_tensor("x_spill", (KT, P, S), F32, kind="Internal").ap())
    args.append(nc.dram_tensor("out_0_dram", (1, S, D), F32, kind="ExternalOutput").ap())
    hybrid_layer(nc, *args)
    r = run(nc, [arrays], core_ids=[0])
    return r.results[0]["out_0_dram"]
```

```python
from contextlib import ExitStack

import concourse.bass as bass
from concourse import mybir

F32 = mybir.dt.float32
F32R = mybir.dt.float32r
ALU = mybir.AluOpType
ACT = mybir.ActivationFunctionType
AX_X = mybir.AxisListType.X

P = 128
D = 1024
S = 1024
KT = D // P
NB = S // P
HALF = 512
HEAD = 64
NQ, NKV = 8, 2
GQA = NQ // NKV
RH = 4
FF = 4 * D
EPS = 1e-6
IN_W = 2816
TK, TV, TQ, RQ, RK, RG, RV = 0, 1, 2, 6, 10, 14, 18
N_PROJ = IN_W // P
N_OUT = D // P
XS = 4
QUARTERS = 4
HK = KT // 2
T_A = N_PROJ
T_B = T_A + N_OUT
T_M = T_B + N_OUT
N_TILES = T_M + QUARTERS * 2 * KT
SLOPES = [2.0 ** (-8.0 * (h + 1) / NQ) for h in range(NQ)]
MASKED = 1e33
C_ID, C_ONE, C_BLK, C_DIST, C_DEC, C_QDEC, C_KDEC = 0, 128, 256, 384, 640, 1152, 1664
C_CHUNK = 1668
C_W = 1672
V_C, V_BADA, V_N1, V_N2, V_RET, V_QG, V_KG, V_ROWS = 0, 8, 56, 64, 72, 76, 77, 78


def shape_constants():
    import numpy as np

    c = np.zeros((P, C_W), np.float64)
    i = np.arange(P)
    c[:, C_ID:C_ID + P] = np.eye(P)
    c[:, C_ONE:C_ONE + P] = 1.0
    c[:, C_BLK:C_BLK + P] = (i[:, None] // HEAD) == (i[None, :] // HEAD)
    dist = i[:, None] + P - np.arange(2 * P)[None, :]
    c[:, C_DIST:C_DIST + 2 * P] = np.where((dist >= 0) & (dist < P), dist, MASKED)
    for h in range(RH):
        lg = np.log1p(-(2.0 ** (-5.0 - h)))
        rel = i[None, :] - i[:, None]
        c[:, C_DEC + h * P:C_DEC + (h + 1) * P] = np.where(rel >= 0, np.exp(lg * np.maximum(rel, 0)), 0) * P ** -0.5
        c[:, C_QDEC + h * P:C_QDEC + (h + 1) * P] = np.exp(lg * (i + 1.0))[None, :]
        c[:, C_KDEC + h] = np.exp(lg * (P - 1.0 - i)) * P ** -0.5
        c[:, C_CHUNK + h] = np.exp(lg * P)
    return c.astype(np.float32)


def hybrid_layer(nc, x, c, norm1_g, norm2_g, w_ada, b_ada, w_in, q_norm_g, k_norm_g, sinks,
                 ret_norm_g, w_out, w_mlp1, w_mlp2, consts, x_spill, out):
    ctx = ExitStack()
    with ctx:
        KB = 1024
        BASE = 16512
        ACTS, REG, WTS, TMP = BASE, BASE + 64 * KB, BASE + 160 * KB, BASE + 184 * KB

        def at(name, shape, off, dt=F32):
            return nc.alloc_sbuf_tensor_at(name, [P] + shape, dt, offset=off)

        act_hi = at("act_hi", [KT, S], ACTS, F32R)
        act_lo = at("act_lo", [KT, S], ACTS + 32 * KB, F32R)
        hn = at("hn", [KT, S], ACTS + 32 * KB)
        proj = at("proj", [N_PROJ, S], REG + 8 * KB)
        x1t = at("x1t", [KT, S], REG)
        hid_hi = at("hid_hi", [KT, S], REG + 32 * KB, F32R)
        hid_lo = at("hid_lo", [KT, S], REG + 64 * KB, F32R)
        w_raw = at("w_raw", [2, KT, P], WTS)
        w_hi = at("w_hi", [2, KT, P], WTS + 8 * KB, F32R)
        w_lo = at("w_lo", [2, KT, P], WTS + 16 * KB, F32R)
        cst = at("cst", [C_W], TMP)
        small = {}
        o = TMP + C_W * 4
        for name, *shape in (("vec", V_ROWS), ("ct", KT), ("ada", 6 * KT), ("a1", KT), ("a2", KT), ("qg8", 1), ("eps", 1),
                             ("ss", NB), ("sd8", NB), ("rs8", NB), ("sink", NQ), ("nsink", NQ),
                             ("mx", 2, 4), ("nm", 2, 4), ("es", 2, 4), ("ex", 2, 4), ("den", 2, 4), ("rd", 2, 4),
                             ("bn", RH, 6), ("mv", RH, 2), ("rsd", RH), ("rri", RH), ("nmr", RH)):
            small[name] = at(name, list(shape), o)
            o += (shape[0] * (shape[1] if len(shape) > 1 else 1) * 4 + 31) // 32 * 32
        vec, ct, ada, a1, a2, qg8, eps, ss, sd8, rs8, sink, nsink = (
            small[k] for k in ("vec", "ct", "ada", "a1", "a2", "qg8", "eps", "ss", "sd8", "rs8", "sink", "nsink"))
        mx, nm, es, ex, den, rd, bn, mv, rsd, rri, nmr = (
            small[k] for k in ("mx", "nm", "es", "ex", "den", "rd", "bn", "mv", "rsd", "rri", "nmr"))
        TMPB = o
        assert TMPB + 16 * KB <= 229368, TMPB + 16 * KB - 229368

        xin = at("xin", [XS, D], REG)
        xt = at("xt", [KT, S], REG + 44 * KB)
        acc = at("acc", [4 * D], REG + 80 * KB)
        wada1 = [at(f"wada1_{k}", [2 * D], off) for k, off in enumerate(
            [REG + (4 * XS + 8 * i) * KB for i in range(3)] + [REG + 88 * KB] + [ACTS + 8 * i * KB for i in range(4)])]
        wada2 = at("wada2", [2, D], REG)
        diag = at("diag", [NB, P], TMPB)
        sqj = at("sqj", [2, D], TMPB + 4 * KB)
        vrow = at("vrow", [P], TMPB + 12 * KB)
        sqb = at("sqb", [2, HALF], TMPB)
        sdq = at("sdq", [2, HALF], TMPB + 4 * KB)
        riq = at("riq", [2, HALF], TMPB + 8 * KB)
        pr = [at("pr0", [GQA, 2 * P], TMPB), at("pr1", [GQA, 2 * P], TMPB + 4 * KB)]
        prt = at("prt", [2, GQA * P], TMPB + 8 * KB)
        vnat = at("vnat", [NB, P], TMPB + 12 * KB)
        kdn = at("kdn", [RH, P], TMPB)
        rvn = at("rvn", [RH, P], TMPB + 2 * KB)
        inn = at("inn", [RH, P], TMPB + 4 * KB)
        inn0 = at("inn0", [RH, P], ACTS + 62 * KB)
        qd = at("qd", [RH, P], TMPB + 6 * KB)
        st = [at(f"st{i}", [RH, P], TMPB + (8 + 2 * i) * KB) for i in range(2)]
        onr = at("onr", [RH, P], TMPB + 12 * KB)
        rvl = at("rvl", [RH, P], TMPB + 14 * KB)
        wo_hi = at("wo_hi", [N_OUT, HK, P], REG + 32 * KB, F32R)
        wo_lo = at("wo_lo", [N_OUT, HK, P], REG + 48 * KB, F32R)
        sq2 = at("sq2", [2, HALF], REG + 80 * KB)
        sqa = at("sqa", [2, HALF], REG + 84 * KB)
        sd2 = at("sd2", [2, HALF], REG + 88 * KB)
        rinv2 = at("rinv2", [2, HALF], REG + 92 * KB)
        ht2 = at("ht2", [2, HALF], REG + 64 * KB)
        rel = at("rel", [S], TMPB)
        rsq = at("rsq", [S], TMPB + 4 * KB)
        fin = at("fin", [S], TMPB + 8 * KB)
        ost = [at("ost0", [NB, P], TMPB + 12 * KB), at("ost1", [NB, P], TMPB)]

        ps = ctx.enter_context(nc.psum_tensor("ps", [P, 8, HALF], F32))
        ident = cst[:, C_ID:C_ID + P]
        ones = cst[:, C_ONE:C_ONE + P]
        blk = cst[:, C_BLK:C_BLK + P]
        dist = cst[:, C_DIST:C_DIST + 2 * P]
        HALVES = [slice(0, HALF), slice(HALF, S)]

        def flat(ap):
            return ap.rearrange("p a b -> p (a b)")

        def bank_pair(slot):
            return flat(ps[:, 2 * slot:2 * slot + 2, :])

        def tile_of(tensor, m):
            return flat(tensor[:, bass.ds(m, 1), :])

        def tokens(n):
            return slice(n * P, (n + 1) * P)

        def sem(name):
            return ctx.enter_context(nc.semaphore(name))

        s_cst, s_vrow, s_sink = sem("consts_loaded"), sem("vectors_loaded"), sem("sinks_loaded")
        s_c, s_id = sem("c_loaded"), sem("identity_loaded")
        s_xin = [sem(f"x_loaded_{n}") for n in range(NB)]
        s_wada1 = [sem(f"w_ada1_loaded_{k}") for k in range(KT + 1)]
        s_wada2 = [sem(f"w_ada2_loaded_{i}") for i in range(2)]
        s_raw = [sem("raw_loaded_0"), sem("raw_loaded_1")]
        s_spill, s_out = sem("x_spilled"), [sem("out_stored_0"), sem("out_stored_1")]
        s_last = sem("last_tile_stored")
        s_back = [sem(f"x_back_{m}") for m in range(KT)]
        s_whi, s_wlo = sem("w_hi_ready"), sem("w_lo_ready")
        s_mmp, s_mma, s_mmb, s_mmm = (sem(n) for n in ("proj_done", "out_a_done", "out_b_done", "mlp_done"))
        s_evp, s_eva, s_evb, s_evm = (sem(n) for n in ("proj_stored", "out_a_added", "out_b_added", "mlp_evacuated"))
        s_vt, s_vec, s_ct = sem("vectors_transposed"), sem("vectors_ready"), sem("c_act_ready")
        s_xtp, s_xt, s_ssq, s_sd = sem("x_transposed"), sem("xt_ready"), sem("x_squares"), sem("x_sd")
        s_diag, s_hnp = sem("diag_ready"), sem("x_scaled_transposed")
        s_acc, s_adat, s_adar = sem("ada_partial_done"), sem("ada_turned"), sem("ada_banks_read")
        s_hn, s_v1, s_hi1, s_act1, s_act1p = (sem("x_over_rms"), sem("modulated"), sem("modulated_hi"),
                                              sem("modulated_lo_by_vector"), sem("modulated_lo_by_pool"))
        s_dve = sem("vector_step")
        s_sqb, s_qss, s_sdq, s_riq, s_qn = (sem("qk_squares"), sem("qk_sums"), sem("qk_sd"), sem("qk_rms_inverse"),
                                            sem("qk_normed"))
        s_gate, s_last0 = sem("ret_gate_ready"), sem("last_proj_first_half_done")
        s_vtr, s_vn = sem("v_transposed"), sem("v_natural")
        s_sc, s_add, s_nm, s_exp, s_pn = (sem("scores_done"), sem("scores_biased"), sem("neg_max_ready"),
                                          sem("exp_done"), sem("probs_ready"))
        s_pt, s_pe, s_pv, s_ao = (sem("probs_transposed"), sem("probs_t_ready"), sem("attention_done"),
                                  sem("attention_stored"))
        s_ahi, s_amix = sem("attention_hi"), sem("attention_split")
        s_rt, s_rvn, s_kdn = sem("ret_kv_transposed"), sem("ret_v_natural"), sem("ret_k_natural")
        s_in, s_inn, s_qd = sem("inner_done"), sem("inner_decayed"), sem("q_decayed")
        s_o, s_kv, s_st = sem("ret_out_done"), sem("ret_kv_done"), sem("state_ready")
        s_var, s_rsd, s_nmr, s_on = sem("ret_var"), sem("ret_sd"), sem("ret_norm_terms"), sem("ret_normed")
        s_ot, s_rvl, s_rhi, s_rmix = sem("ret_transposed"), sem("ret_gated"), sem("ret_hi"), sem("ret_split")
        s_sq2, s_sqa, s_ss2, s_sd2 = sem("x1_squares"), sem("x1_squares_summed"), sem("x1_sums"), sem("x1_sd")
        s_h2, s_hi2, s_act2 = sem("normed2"), sem("normed2_hi"), sem("normed2_split")
        s_rsq, s_hih, s_hid = sem("relu_squared"), sem("hidden_hi"), sem("hidden_ready")
        s_half, s_ftr, s_ost = sem("last_half_done"), sem("final_transposed"), sem("out_staged")

        out_t = out[0].rearrange("(b p) n -> p b n", p=P)
        block = ctx.enter_context(nc.Block())

        def wait(eng, s, v):
            if not isinstance(v, int) or v > 0:
                eng.wait_ge(s, v)

        def wait_used(eng, t, mlp=False):
            if mlp or (isinstance(t, int) and t >= T_M):
                eng.wait_ge(s_mmm, t - (T_M - 1))
            elif t >= T_A:
                eng.wait_ge(s_mma, 3 if t == T_A else 2 * min(t - T_A + 1, N_OUT))
            elif t >= 0:
                eng.wait_ge(s_mmp, t + 1)

        def n_loads(t):
            return 2 if TQ <= t < TQ + GQA or T_A <= t < T_B else 1

        def loaded(t):
            return 16 * sum(n_loads(v) for v in range(t % 2, t + 1, 2))

        def k_tiles(t):
            return HK if isinstance(t, int) and T_A <= t < T_M else KT

        def pairs(eng, t0, n, step):
            assert t0 >= T_M and t0 + 2 * n < N_TILES
            with eng.Fori(0, n) as i:
                for s in range(2):
                    step(i * 2 + (t0 + s), s, i * 16 + loaded(t0 + s + 1))

        ACC1 = KT + 1

        NU = NB * NKV
        T_ATT = TQ + GQA
        ADA_OPS = 2
        ADA_TURN = {KT * (j + 1) // ADA_OPS + 1: j for j in range(4)}
        assert max(ADA_TURN) < RV and NU == N_PROJ - T_ATT

        OUT_A = [(0, 0), (1, 0), (0, 1), (1, 1)] + [(m, half) for m in range(2, N_OUT) for half in range(2)]

        NORM2_UNITS = {N_OUT + 2: 1, N_OUT + 3: 2, N_OUT + 4: 1, N_OUT + 5: 1, N_OUT + 6: 1, N_OUT + 7: 2}
        assert sum(NORM2_UNITS.values()) == KT

        @block.sync
        def _(sp):
            sp.dma_start(vrow[V_C:V_C + KT, :], c.rearrange("b (t p) -> (b t) p", p=P)).then_inc(s_c, 16)
            sp.dma_start(cst[:, 0:C_ONE], consts[:, 0:C_ONE]).then_inc(s_id, 16)
            for k in range(KT):
                for n in range(2 * k, min(2 * k + 2, NB)):
                    if n >= XS:
                        sp.wait_ge(s_hnp, n - XS + 1)
                        sp.wait_ge(s_xtp, n - XS + 1)
                        sp.wait_ge(s_ssq, n - XS + 1)
                    sp.dma_start(xin[:, n % XS, :], x[0, n * P:(n + 1) * P, :]).then_inc(s_xin[n], 16)
                if k < KT - 1:
                    sp.dma_start(wada1[k][:, :], w_ada[0, k * P:(k + 1) * P, 0:2 * D]).then_inc(s_wada1[k], 16)
            for j in (1, 0):
                sp.dma_start(wada1[KT - 1][:, j * D:(j + 1) * D],
                             w_ada[0, (KT - 1) * P:KT * P, j * D:(j + 1) * D]).then_inc(s_wada1[KT - j], 16)

            w_in_k = w_in[0].rearrange("(k p) n -> p k n", p=P)
            w_in_q = w_in[0][:, 0:NQ * HEAD].rearrange("(k p) (g n) -> p k g n", p=P, g=NKV)
            w_out_q = w_out[0][0:NQ * HEAD, :].rearrange("(g k d) n -> g d k n", g=NKV, k=GQA)
            w_out_r = w_out[0][NQ * HEAD:, :].rearrange("(k p) n -> p k n", p=P)
            w1_k = w_mlp1[0].rearrange("(k p) n -> p k n", p=P)
            w2_k = w_mlp2[0].rearrange("(q k p) n -> p q k n", p=P, q=QUARTERS)

            def load(slot, src, ks=KT):
                sp.dma_start(w_raw[:, slot, 0:ks, :], src).then_inc(s_raw[slot], 16)

            for t in range(T_M):
                wait(sp, s_wlo, t - 1)
                if TQ <= t < TQ + GQA:
                    for g in range(NKV):
                        col = (t - TQ) * HEAD
                        sp.dma_start(w_raw[:, t % 2, :, g * HEAD:(g + 1) * HEAD],
                                     w_in_q[:, :, g, col:col + HEAD]).then_inc(s_raw[t % 2], 16)
                elif t < N_PROJ:
                    col = NQ * HEAD + t * P if t < TQ else (t + RH) * P if RG <= t < RV else (
                        t - RH) * P if t >= RV else t * P
                    load(t % 2, w_in_k[:, :, col:col + P])
                elif t < T_B:
                    for g in range(NKV):
                        sp.dma_start(w_raw[g * HEAD:(g + 1) * HEAD, t % 2, 0:HK, :],
                                     w_out_q[g][:, :, tokens(t - T_A)]).then_inc(s_raw[t % 2], 16)
                else:
                    load(t % 2, w_out_r[:, :, tokens(t - T_B)], HK)
                if t == 1:
                    sp.dma_start(cst[:, C_ONE:], consts[:, C_ONE:]).then_inc(s_cst, 16)
            for q in range(QUARTERS):
                for first, src in ((T_M + q * 2 * KT, w1_k[:, :, q * D:(q + 1) * D]),
                                   (T_M + (q * 2 + 1) * KT, w2_k[:, q, :, :])):
                    with sp.Fori(0, KT // 2) as i:
                        for s in range(2):
                            sp.wait_ge(s_wlo, i * 2 + (first + s - 1))
                            load(s, src[:, :, bass.ds(i * 2 * P + s * P, P)])
            for half in range(2):
                sp.wait_ge(s_ost, KT + half)
                blocks = slice(half * NB // 2, (half + 1) * NB // 2)
                sp.dma_start(out_t[:, blocks, tokens(KT - 1)], ost[1][:, blocks, :]).then_inc(s_last, 16)
            sp.wait_ge(s_last, 32)

        @block.gpsimd
        def _(pool):
            pool.dma_start(vrow[V_BADA:V_BADA + 48, :], b_ada.rearrange("l (t p) -> (l t) p", p=P)).then_inc(s_vrow, 16)
            pool.dma_start(vrow[V_N1:V_N1 + KT, :], norm1_g.rearrange("l (t p) -> (l t) p", p=P)).then_inc(s_vrow, 16)
            pool.dma_start(vrow[V_N2:V_N2 + KT, :], norm2_g.rearrange("l (t p) -> (l t) p", p=P)).then_inc(s_vrow, 16)
            pool.dma_start(vrow[V_RET:V_RET + RH, :], ret_norm_g.rearrange("l (t p) -> (l t) p", p=P)).then_inc(s_vrow, 16)
            for row, g in ((V_QG, q_norm_g), (V_KG, k_norm_g)):
                for half in range(2):
                    pool.dma_start(vrow[row:row + 1, half * HEAD:(half + 1) * HEAD], g).then_inc(s_vrow, 16)
            pool.dma_start(sink[:, :], sinks[0].partition_broadcast(P)).then_inc(s_sink, 16)

            pool.wait_ge(s_vec, 1)
            pool.tensor_scalar(qg8[:, :], vec[:, V_QG:V_QG + 1], HEAD ** -0.5, None, ALU.mult).then_inc(s_vec, 1)
            pool.wait_ge(s_sink, 16)
            pool.tensor_scalar(nsink[:, :], sink[:, :], -1.0, None, ALU.mult).then_inc(s_vec, 1)

            for t in range(2):
                pool.wait_ge(s_whi, t + 1)
                pool.tensor_tensor(w_lo[:, t, :, :], w_raw[:, t, :, :], w_hi[:, t, :, :].bitcast(F32),
                                   ALU.subtract).then_inc(s_wlo, 1)
            for u in range(3, 2 * KT, 4):
                half, k = divmod(u, KT)
                cols = HALVES[half]
                pool.wait_ge(s_hi1, u + 1)
                pool.tensor_tensor(act_lo[:, k, cols], hn[:, k, cols], act_hi[:, k, cols].bitcast(F32),
                                   ALU.subtract).then_inc(s_act1p, 1)
            def load_ada2(u):
                j, k = divmod(u, KT)
                if u >= 2:
                    pool.wait_ge(s_acc, ACC1 + u - 1)
                pool.dma_start(wada2[:, u % 2, :],
                               w_ada[0, k * P:(k + 1) * P, (2 + j) * D:(3 + j) * D]).then_inc(s_wada2[u % 2], 16)

            pool.wait_ge(s_hnp, NB)
            pool.wait_ge(s_ssq, NB)
            pool.wait_ge(s_xt, NB)
            for u in range(4 * KT):
                load_ada2(u)
                if 2 <= u < KT + 2:
                    pool.dma_start(x_spill[u - 2], xt[:, u - 2, :]).then_inc(s_spill, 16)

            def back(m):
                pool.dma_start(x1t[:, m, :], x_spill[m]).then_inc(s_back[m], 16)

            pool.wait_ge(s_spill, 16 * KT)
            pool.wait_ge(s_acc, ACC1 + 4 * KT)
            back(0)
            back(1)
            pool.wait_ge(s_vtr, 1)
            back(3)
            pool.wait_ge(s_sc, NU)
            back(2)

            def q_decayed(n):
                wait(pool, s_o, n)
                pool.tensor_tensor(qd[:, :, :], proj[:, RQ:RQ + RH, tokens(n)],
                                   cst[:, C_QDEC:C_QDEC + RH * P].rearrange("p (h n) -> p h n", h=RH),
                                   ALU.mult).then_inc(s_qd, 1)

            pool.wait_ge(s_evp, RQ + RH)
            for m in range(4, KT):
                pool.wait_ge(s_amix, HK + m - 3)
                back(m)
            pool.wait_ge(s_pt, NU)
            for n in range(1, NB):
                q_decayed(n)
            for half in range(2):
                for m in range(KT):
                    u = half * KT + m
                    pool.wait_ge(s_sq2, u + 1)
                    if m:
                        pool.wait_ge(s_sqa, u)
                        pool.tensor_tensor(sqa[:, half, :], sqa[:, half, :], sq2[:, u % 2, :], ALU.add).then_inc(s_sqa, 1)
                    else:
                        pool.tensor_copy(sqa[:, half, :], sq2[:, u % 2, :]).then_inc(s_sqa, 1)
            for m in range(KT - 1):
                pool.wait_ge(s_ost, m + 1)
                pool.dma_start(out_t[:, :, tokens(m)], ost[m % 2][:, :, :]).then_inc(s_out[m % 2], 16)
            pool.wait_ge(s_out[0], 16 * KT // 2)
            pool.wait_ge(s_out[1], 16 * (KT // 2 - 1))

        @block.tensor
        def _(pe):
            def passes(bank, wh, wl, hi, lo, first, last):
                pe.matmul(bank, wh, hi, start=first, stop=False)
                pe.matmul(bank, wh, lo, start=False, stop=False)
                return pe.matmul(bank, wl, hi, start=False, stop=last)

            def chain(bank, slot, hi, lo, cols, ks, koff=0, before=None, wh=w_hi, wl=w_lo):
                for k in range(ks):
                    if before is not None:
                        before(k)
                    mm = passes(bank, wh[:, slot, k, :], wl[:, slot, k, :], hi[:, koff + k, cols], lo[:, koff + k, cols],
                                k == 0, k == ks - 1)
                return mm

            def both_tiles(half, part_there, lag=0, done=None):
                for step in range(KT + lag):
                    for s, k in ((0, step), (1, step - lag)):
                        if not 0 <= k < KT:
                            continue
                        if s == 0:
                            part_there(half * KT + k)
                        mm = passes(ps[:, 2 * s + half, :], w_hi[:, s, k, :], w_lo[:, s, k, :], act_hi[:, k, HALVES[half]],
                                    act_lo[:, k, HALVES[half]], k == 0, k == KT - 1)
                        if done is not None and k == KT - 1:
                            mm.then_inc(done, 1)

            pe.wait_ge(s_c, 16)
            pe.wait_ge(s_id, 16)
            pe.transpose(ps[:, 6, 0:KT], vrow[V_C:V_C + KT, :], cst[0:KT, C_ID:C_ID + KT]).then_inc(s_vt, 1)
            for n in range(NB + 1):
                if n < NB:
                    pe.wait_ge(s_xin[n], 16)
                    wait(pe, s_xt, n - 1)
                    for k in range(KT):
                        tr = pe.transpose(ps[:, 2 * (n % 2) + k // 4, tokens(k % 4)], xin[:, n % XS, tokens(k)], ident)
                    tr.then_inc(s_xtp, 1)
                if n:
                    pe.wait_ge(s_diag, n)
                    wait(pe, s_hn, n - 2)
                    if n == 2:
                        pe.wait_ge(s_ct, 1)
                    for k in range(KT):
                        mm = pe.matmul(ps[:, 4 + 2 * ((n - 1) % 2) + k // 4, tokens(k % 4)],
                                       xin[:, (n - 1) % XS, tokens(k)], diag[:, n - 1, :], start=True, stop=True)
                    mm.then_inc(s_hnp, 1)
            pe.wait_ge(s_vrow, 16 * 8)
            pe.wait_ge(s_hn, NB)
            pe.transpose(ps[:, 7, 0:V_ROWS], vrow[0:V_ROWS, :], cst[0:V_ROWS, C_ID:C_ID + V_ROWS]).then_inc(s_vt, 1)

            def ada_turn(j, bank):
                for m in range(KT):
                    tr = pe.transpose(ps[:, bank + m // 4, tokens(m % 4)],
                                      acc[:, j * D + m * P:j * D + (m + 1) * P], ident)
                tr.then_inc(s_adat, 1)

            pe.wait_ge(s_xt, NB)
            for i, j in enumerate((1, 0)):
                pe.wait_ge(s_acc, KT + i)
                ada_turn(j, 2 * j)

            def qk_sums(tile):
                i = 0 if tile == TK else tile - TQ + 1
                for half in range(2):
                    u = 2 * i + half
                    pe.wait_ge(s_sqb, u + 1)
                    wait(pe, s_sdq, u - 1)
                    pe.matmul(ps[:, 4 + half, :], blk, sqb[:, half, :], start=True, stop=True).then_inc(s_qss, 1)

            def turn_v():
                pe.wait_ge(s_evp, TV + 1)
                for n in range(NB):
                    tr = pe.transpose(ps[:, 6 + n // 4, (n % 4) * P:(n % 4 + 1) * P], proj[:, TV, tokens(n)], ident)
                tr.then_inc(s_vtr, 1)

            def scores(u):
                n, g = divmod(u, NKV)
                rows = slice(g * HEAD, (g + 1) * HEAD)
                lo = 0 if n else P
                if u == 0:
                    pe.wait_ge(s_qn, 10)
                wait(pe, s_add, u)
                for p in range(GQA):
                    mm = pe.matmul(ps[:, 4 + p // 2, (p % 2) * 256 + lo:(p % 2) * 256 + 256],
                                   proj[rows, TQ + p, tokens(n)],
                                   proj[rows, TK, (n - 1) * P + lo:(n + 1) * P], start=True, stop=True)
                mm.then_inc(s_sc, 1)

            def probs_turn(u):
                blocks = (0, 1) if u >= NKV else (1,)
                pe.wait_ge(s_pn, u + 1)
                wait(pe, s_ao, u)
                pe.wait_ge(s_adar, 2 + sum(T_ATT + u + 1 >= t for t in ADA_TURN))
                for b in blocks:
                    for p in range(GQA):
                        tr = pe.transpose(ps[:, 6 + b, tokens(p)], pr[u % 2][:, p, b * P:(b + 1) * P], ident)
                tr.then_inc(s_pt, 1)

            def attend(u):
                n, g = divmod(u, NKV)
                pe.wait_ge(s_pe, u + 1)
                if u == 0:
                    pe.wait_ge(s_vn, 1)
                for b in ((0, 1) if n else (1,)):
                    mm = pe.matmul(ps[g * HEAD:(g + 1) * HEAD, 6, :], vnat[:, n - 1 + b, g * HEAD:(g + 1) * HEAD],
                                   prt[:, b, :], start=(b == 0 or n == 0), stop=(b == 1))
                mm.then_inc(s_pv, 1)

            pe.wait_ge(s_wlo, 2)
            pe.wait_ge(s_adar, 2)

            def unit_there(un):
                if un % 4 == 3:
                    pe.wait_ge(s_act1p, un // 4 + 1)
                else:
                    pe.wait_ge(s_act1, un - un // 4 + 1)

            both_tiles(0, unit_there)
            for t in range(2):
                def before(k):
                    if t == 0:
                        unit_there(KT + k)
                    if (t, k) == (1, 7):
                        pe.wait_ge(s_cst, 16)
                        qk_sums(TK)
                chain(ps[:, 2 * t + 1, :], t, act_hi, act_lo, HALVES[1], KT, 0, before).then_inc(s_mmp, 1)
            for t in range(2, N_PROJ):
                slot, u = t % 2, t - T_ATT
                pe.wait_ge(s_wlo, t + 1)
                pe.wait_ge(s_evp, t - 1)
                for half in range(2):
                    def before(k):
                        if (half, k) == (0, 4) and t <= T_ATT and t - 1 != TV:
                            qk_sums(t - 1)
                        if (half, k) == (0, 5) and t == TV + 2:
                            turn_v()
                        if (half, k) == (0, 4) and t in ADA_TURN:
                            j = ADA_TURN[t]
                            pe.wait_ge(s_acc, ACC1 + KT * (j + 1))
                            pe.wait_ge(s_vn, 1)
                            wait(pe, s_ao, u - 1)
                            ada_turn(j, 6)
                        if (half, k) == (1, 4) and u >= 1:
                            probs_turn(u - 1)
                    mm = chain(ps[:, 2 * slot + half, :], slot, act_hi, act_lo, HALVES[half], KT, 0, before)
                    if (t, half) == (N_PROJ - 1, 0):
                        mm.then_inc(s_last0, 1)
                mm.then_inc(s_mmp, 1)
                if u >= 1:
                    attend(u - 1)
                if u >= 0:
                    scores(u)

            def ret_in(n):
                wait(pe, s_kdn, n)
                wait(pe, s_rvn, n)
                for h in range(RH):
                    pe.transpose(ps[:, 2, tokens(h)], proj[:, RK + h, tokens(n)], ident)
                for h in range(RH):
                    tr = pe.transpose(ps[:, 3, tokens(h)], proj[:, RV + h, tokens(n)], ident)
                tr.then_inc(s_rt, 1)
                wait(pe, s_inn, n)
                if n == 0:
                    pe.wait_ge(s_add, NU)
                for h in range(RH):
                    mm = pe.matmul(ps[:, 4, tokens(h)], proj[:, RK + h, tokens(n)], proj[:, RQ + h, tokens(n)],
                                   start=True, stop=True)
                mm.then_inc(s_in, 1)

            def ret_kv(n):
                pe.wait_ge(s_kdn, n + 1)
                pe.wait_ge(s_rvn, n + 1)
                wait(pe, s_st, n)
                for h in range(RH):
                    mm = pe.matmul(ps[:, 6, tokens(h)], kdn[:, h, :], rvn[:, h, :], start=True, stop=True)
                mm.then_inc(s_kv, 1)

            def ret_out(n):
                pe.wait_ge(s_rvn, n + 1)
                pe.wait_ge(s_inn, n + 1)
                if n:
                    pe.wait_ge(s_qd, n)
                    pe.wait_ge(s_st, n)
                wait(pe, s_on, n)
                for h in range(RH):
                    bank = ps[:, 5, tokens(h)]
                    mm = pe.matmul(bank, (inn if n else inn0)[:, h, :], rvn[:, h, :], start=True, stop=(n == 0))
                    if n:
                        mm = pe.matmul(bank, qd[:, h, :], st[n % 2][:, h, :], start=False, stop=True)
                mm.then_inc(s_o, 1)

            def ret_turn(n):
                pe.wait_ge(s_on, n + 1)
                wait(pe, s_rvl, n)
                for h in range(RH):
                    tr = pe.transpose(ps[:, 7, tokens(h)], onr[:, h, :], ident)
                tr.then_inc(s_ot, 1)

            for i, (m, half) in enumerate(OUT_A):
                if half == 0 or i < 4:
                    pe.wait_ge(s_wlo, T_A + m + 1)
                if i == 0:
                    pe.wait_ge(s_evp, N_PROJ - 1)
                wait(pe, s_eva, i - 1)

                def before(k):
                    if m == 0:
                        pe.wait_ge(s_amix, half * HK + k + 1)
                chain(ps[:, i % 2, :], m % 2, act_hi, act_lo, HALVES[half], HK, 0, before).then_inc(s_mma, 1)
                if i == 0:
                    pe.wait_ge(s_evp, N_PROJ)
                    ret_in(0)
                elif i % 2:
                    n = (i + 1) // 2
                    if n == 1:
                        ret_out(0)
                        probs_turn(NU - 1)
                        ret_in(1)
                        attend(NU - 1)
                        pe.wait_ge(s_ao, NU)
                        ret_kv(0)
                        continue
                    ret_turn(n - 2)
                    if n < NB:
                        ret_kv(n - 1)
                    ret_out(n - 1)
                    if n < NB:
                        ret_in(n)

            def x1_sums(half):
                pe.wait_ge(s_sqa, (half + 1) * KT)
                wait(pe, s_sd2, half)
                pe.matmul(ps[:, 4, :], ones, sqa[:, half, :], start=True, stop=True).then_inc(s_ss2, 1)

            for b in range(2 * N_OUT):
                half, m = divmod(b, N_OUT)
                if half == 0:
                    pe.wait_ge(s_wlo, T_B + m + 1)
                if b < 2:
                    pe.wait_ge(s_eva, 2 * N_OUT - 1 + b)
                elif b < 4:
                    pe.wait_ge(s_kdn if b == 2 else s_rvn, NB)
                wait(pe, s_evb, b - 3)
                if b == 0:
                    pe.wait_ge(s_rmix, NB // 2)
                if b == N_OUT:
                    pe.wait_ge(s_rmix, NB)

                def before(k):
                    if (b, k) == (N_OUT + 1, 1):
                        x1_sums(0)
                chain(ps[:, b % 4, :], m, act_hi, act_lo, HALVES[half], HK, HK, before, wo_hi, wo_lo).then_inc(s_mmb, 1)
                if b == 2:
                    ret_turn(NB - 1)

            def product(t, slot, hi, lo, before=None):
                pe.wait_ge(s_wlo, t + 1)
                pe.wait_ge(s_evm, t - (T_M + 1))
                for half in range(2):
                    mm = chain(ps[:, 2 * slot + half, :], slot, hi, lo, HALVES[half], KT, 0,
                               (lambda k: before(half, k)) if before else None)
                mm.then_inc(s_mmm, 1)

            pe.wait_ge(s_wlo, T_M + 2)
            pe.wait_ge(s_evb, 2 * N_OUT - 1)

            def part_there(u):
                pe.wait_ge(s_act2, u + 1)
                if u == 2:
                    pe.wait_ge(s_evb, 2 * N_OUT)
                    x1_sums(1)
            both_tiles(0, part_there)
            both_tiles(1, part_there, 2, s_mmm)
            for q in range(QUARTERS):
                t0 = T_M + q * 2 * KT
                with pe.Fori(1 if q == 0 else 0, KT // 2) as i:
                    for s in range(2):
                        product(i * 2 + (t0 + s), s, act_hi, act_lo)
                t1 = t0 + KT
                product(t1, 0, hid_hi, hid_lo, lambda half, k: pe.wait_ge(s_hid, q * KT + k + 1) if half == 0 else None)
                product(t1 + 1, 1, hid_hi, hid_lo)
                if q < QUARTERS - 1:
                    with pe.Fori(1, KT // 2) as i:
                        for s in range(2):
                            product(i * 2 + (t1 + s), s, hid_hi, hid_lo)

            def turn(m, halves=(0, 1), evacuated=0):
                pe.wait_ge(s_evm, m + (N_TILES - KT - T_M + 1 + evacuated))
                wait(pe, s_ost, m)
                for half in halves:
                    for n in range(NB // 2):
                        tr = pe.transpose(ps[:, 4 + half, tokens(n)], fin[:, tokens(half * NB // 2 + n)], ident)
                tr.then_inc(s_ftr, 1)

            turn(0)
            with pe.Fori(1, KT // 2 - 1) as i:
                for s in range(2):
                    product(i * 2 + (t1 + s), s, hid_hi, hid_lo)
                    turn(i * 2 + (s - 1))
            product(N_TILES - 2, 0, hid_hi, hid_lo)
            turn(KT - 3)
            pe.wait_ge(s_wlo, N_TILES)
            pe.wait_ge(s_evm, N_TILES - T_M - 2)
            chain(ps[:, 2, :], 1, hid_hi, hid_lo, HALVES[0], KT).then_inc(s_half, 1)

            def before(k):
                if k == 0:
                    turn(KT - 2)
                if k == 5:
                    turn(KT - 1, (0,))
            chain(ps[:, 3, :], 1, hid_hi, hid_lo, HALVES[1], KT, 0, before).then_inc(s_half, 1)
            turn(KT - 1, (1,), 1)

        @block.scalar
        def _(act):
            def split_hi(t, slot, count, mlp=False):
                ks = k_tiles(t)
                act.wait_ge(s_raw[slot], count)
                if isinstance(t, int) and T_B <= t < T_M:
                    act.activation(wo_hi[:, t - T_B, :, :], w_raw[:, slot, 0:ks, :], ACT.Copy).then_inc(s_whi, 1)
                    return
                wait_used(act, t - 2, mlp)
                act.activation(w_hi[:, slot, 0:ks, :], w_raw[:, slot, 0:ks, :], ACT.Copy).then_inc(s_whi, 1)

            def split_next(t):
                split_hi(t + 1, (t + 1) % 2, loaded(t + 1))

            act.wait_ge(s_vt, 1)
            act.activation(ct[:, :], ps[:, 6, 0:KT], ACT.Silu).then_inc(s_ct, 1)
            act.wait_ge(s_dve, 1)
            for n in range(NB + 1):
                if n < NB:
                    act.wait_ge(s_xin[n], 16)
                    wait(act, s_ssq, n - 1)
                    act.activation(sqj[:, n % 2, :], xin[:, n % XS, :], ACT.Square,
                                   accum_out=ss[:, n:n + 1]).then_inc(s_ssq, 1)
                    act.wait_ge(s_ssq, n + 1)
                    act.activation(sd8[:, n:n + 1], ss[:, n:n + 1], ACT.Sqrt, bias=eps[:, :], scale=1.0 / D).then_inc(s_sd, 1)
                    act.wait_ge(s_xtp, n + 1)
                    act.activation(xt[:, :, tokens(n)], bank_pair(n % 2).rearrange("p (k n) -> p k n", k=KT),
                                   ACT.Copy).then_inc(s_xt, 1)
                if n:
                    act.wait_ge(s_hnp, n)
                    act.activation(hn[:, :, tokens(n - 1)],
                                   bank_pair(2 + (n - 1) % 2).rearrange("p (k n) -> p k n", k=KT), ACT.Copy).then_inc(s_hn, 1)
            act.wait_ge(s_vt, 2)
            act.activation(vec[:, :], ps[:, 7, 0:V_ROWS], ACT.Copy).then_inc(s_vec, 1)
            split_next(-1)
            split_next(0)
            for u in range(2 * KT):
                half, k = divmod(u, KT)
                act.wait_ge(s_v1, u + 1)
                act.activation(act_hi[:, k, HALVES[half]], hn[:, k, HALVES[half]], ACT.Copy).then_inc(s_hi1, 1)

            def qk_sd(tile):
                i = 0 if tile == TK else tile - TQ + 1
                for half in range(2):
                    u = 2 * i + half
                    act.wait_ge(s_qss, u + 1)
                    wait(act, s_riq, u - 1)
                    act.activation(sdq[:, half, :], ps[:, 4 + half, :], ACT.Sqrt, bias=eps[:, :],
                                   scale=1.0 / HEAD).then_inc(s_sdq, 1)

            def exps(u):
                i, lo = u % 2, 0 if u >= NKV else P
                act.wait_ge(s_nm, u + 1)
                for p in range(GQA):
                    act.activation(pr[i][:, p, lo:], pr[i][:, p, lo:], ACT.Exp, bias=nm[:, i, p:p + 1],
                                   accum_out=den[:, i, p:p + 1])
                act.activation(ex[:, i, :], es[:, i, :], ACT.Exp).then_inc(s_exp, 1)

            def probs_copy(u):
                b0 = 0 if u >= NKV else 1
                act.wait_ge(s_pt, u + 1)
                wait(act, s_pv, u)
                act.activation(prt[:, b0:, :], ps[:, 6 + b0:8, :], ACT.Copy).then_inc(s_pe, 1)

            def attn_store(u):
                n, g = divmod(u, NKV)
                rows = slice(g * HEAD, (g + 1) * HEAD)
                act.wait_ge(s_pv, u + 1)
                act.activation(proj[rows, TQ:TQ + GQA, tokens(n)], ps[rows, 6, :].rearrange("p (k n) -> p k n", k=GQA),
                               ACT.Copy).then_inc(s_ao, 1)

            def attn_hi(half):
                for k in range(HK):
                    act.wait_ge(s_ao, (half + 1) * NU // 2)
                    act.activation(act_hi[:, k, HALVES[half]], proj[:, TQ + k, HALVES[half]], ACT.Copy).then_inc(s_ahi, 1)

            for t in range(N_PROJ):
                u = t - T_ATT
                if u >= 1:
                    exps(u - 1)
                if 0 < t < T_ATT:
                    split_next(t)
                if 0 < t <= T_ATT and t - 1 != TV:
                    qk_sd(t - 1)
                if t >= T_ATT:
                    split_next(t)
                if t == TV + 2:
                    act.wait_ge(s_vtr, 1)
                    act.activation(flat(vnat[:, :, :]), flat(ps[:, 6:8, :]), ACT.Copy).then_inc(s_vn, 1)
                if u >= 1:
                    probs_copy(u - 1)
                if t == 9:
                    act.wait_ge(s_spill, 16 * KT)
                if t == RV:
                    act.wait_ge(s_adat, 6)
                if t == N_PROJ - 1:
                    act.wait_ge(s_last0, 1)
                    attn_hi(0)
                act.wait_ge(s_mmp, t + 1)
                act.activation(proj[:, t, :], bank_pair(t % 2), ACT.Silu if RG <= t < RV else ACT.Copy).then_inc(s_evp, 1)
                if t < T_ATT and t != TV:
                    i = 0 if t == TK else t - TQ + 1
                    wait(act, s_qss, 2 * i)
                    act.wait_ge(s_evp, t + 1)
                    for half in range(2):
                        act.activation(sqb[:, half, :], proj[:, t, HALVES[half]], ACT.Square).then_inc(s_sqb, 1)
                if u >= 1:
                    attn_store(u - 1)


            def ret_v(n):
                act.wait_ge(s_rt, n + 1)
                wait(act, s_o, n)
                wait(act, s_kv, n)
                act.activation(flat(rvn[:, :, :]), ps[:, 3, :], ACT.Copy).then_inc(s_rvn, 1)

            def ret_hi(n):
                act.wait_ge(s_rvl, n + 1)
                act.activation(act_hi[:, HK:, tokens(n)], rvl[:, :, :], ACT.Copy).then_inc(s_rhi, 1)

            def ret_norm(n):
                act.wait_ge(s_var, n + 1)
                act.activation(rsd[:, :], mv[:, :, 1], ACT.Sqrt, bias=eps[:, :]).then_inc(s_rsd, 1)
                act.wait_ge(s_nmr, n + 1)
                wait(act, s_ot, n)
                for h in range(RH):
                    on = act.activation(onr[:, h, :], ps[:, 5, tokens(h)], ACT.Identity,
                                        bias=nmr[:, h:h + 1], scale=rri[:, h:h + 1])
                on.then_inc(s_on, 1)

            split_next(T_A)
            ret_v(0)
            exps(NU - 1)
            probs_copy(NU - 1)
            attn_store(NU - 1)
            attn_hi(1)
            for n in range(1, NB + 1):
                if 1 < n < N_OUT - 1 or n == NB:
                    split_next(T_A + n)
                if n >= 2:
                    ret_hi(n - 2)
                if n < NB:
                    ret_v(n)
                if n == N_OUT - 1:
                    act.wait_ge(s_in, NB)
                    act.wait_ge(s_qd, NB - 1)
                    split_next(T_A + n)
                ret_norm(n - 1)
                if n == 1:
                    split_next(T_A + n)

            unit = [0]

            def norm2_sd(half):
                act.wait_ge(s_ss2, half + 1)
                act.activation(sd2[:, half, :], ps[:, 4, :], ACT.Sqrt, bias=eps[:, :], scale=1.0 / D).then_inc(s_sd2, 1)

            def norm2_hi():
                half, k = divmod(unit[0], KT)
                act.wait_ge(s_h2, unit[0] + 1)
                act.activation(act_hi[:, k, HALVES[half]], ht2[:, unit[0] % 2, :], ACT.Identity,
                               bias=ada[:, 3 * KT + k:3 * KT + k + 1]).then_inc(s_hi2, 1)
                unit[0] += 1

            for b in range(2 * N_OUT):
                half, m = divmod(b, N_OUT)
                if 1 <= b <= N_OUT:
                    split_next(T_B + b)
                if b == 2:
                    ret_hi(NB - 1)
                act.wait_ge(s_evb, b + 1)
                wait(act, s_sqa, b - 1)
                act.activation(sq2[:, b % 2, :], x1t[:, m, HALVES[half]], ACT.Square).then_inc(s_sq2, 1)
                if b == N_OUT + 1:
                    norm2_sd(0)
                for _ in range(NORM2_UNITS.get(b, 0)):
                    norm2_hi()
            norm2_sd(1)
            for _ in range(KT):
                norm2_hi()

            def up(q):
                t0 = T_M + q * 2 * KT

                def step(t, slot, count):
                    split_hi(t + 1, 1 - slot, count, mlp=True)
                    relu_split(t, slot, t - t0, q)
                return step

            def relu_split(t, slot, m, q):
                act.wait_ge(s_mmm, t - (T_M - 1))
                wait(act, s_rsq, m + q * KT)
                act.activation(rel[:, :], bank_pair(slot), ACT.Relu).then_inc(s_evm, 1)
                act.wait_ge(s_rsq, m + (q * KT + 1))
                act.activation(tile_of(hid_hi, m), rsq[:, :], ACT.Copy).then_inc(s_hih, 1)

            def down(t, slot, count):
                split_hi(t + 1, 1 - slot, count, mlp=True)

            for q in range(QUARTERS):
                t0 = T_M + q * 2 * KT
                if q == 0:
                    split_hi(t0 + 2, 0, loaded(t0 + 2), mlp=True)
                    relu_split(t0, 0, 0, 0)
                    relu_split(t0 + 1, 1, 1, 0)
                    pairs(act, t0 + 2, KT // 2 - 1, up(0))
                else:
                    pairs(act, t0, KT // 2, up(q))
                if q < QUARTERS - 1:
                    pairs(act, t0 + KT, KT // 2, down)

            def stage(m, slot):
                act.wait_ge(s_ftr, m + 1)
                if not isinstance(m, int) or m >= 2:
                    act.wait_ge(s_out[slot], (m - slot) * 8)
                act.activation(flat(ost[slot][:, :, :]), flat(ps[:, 4:6, :]), ACT.Copy).then_inc(s_ost, 1)

            t1 = N_TILES - KT
            for m in range(KT - 1):
                down(t1 + m, m % 2, loaded(t1 + m + 1))
                if m:
                    stage(m - 1, (m - 1) % 2)
            stage(KT - 2, 0)
            for half in range(2):
                act.wait_ge(s_ftr, KT + half)
                if half == 0:
                    act.wait_ge(s_out[1], 16 * (KT // 2 - 1))
                act.activation(flat(ost[1][:, half * NB // 2:(half + 1) * NB // 2, :]), ps[:, 4 + half, :],
                               ACT.Copy).then_inc(s_ost, 1)

        @block.vector
        def _(dve):
            own = [0]

            def link(ins):
                own[0] += 1
                ins.then_inc(s_dve, 1)
                dve.wait_ge(s_dve, own[0])

            def split_lo(t, slot):
                ks = k_tiles(t)
                dve.wait_ge(s_whi, t + 1)
                if isinstance(t, int) and T_B <= t < T_M:
                    m = t - T_B
                    dve.tensor_tensor(wo_lo[:, m, :, :], w_raw[:, slot, 0:ks, :], wo_hi[:, m, :, :].bitcast(F32),
                                      ALU.subtract).then_inc(s_wlo, 1)
                    return
                dve.tensor_tensor(w_lo[:, slot, 0:ks, :], w_raw[:, slot, 0:ks, :], w_hi[:, slot, 0:ks, :].bitcast(F32),
                                  ALU.subtract).then_inc(s_wlo, 1)

            def split_next(t):
                split_lo(t + 1, (t + 1) % 2)

            link(dve.memset(eps[:, :], EPS))
            def ada_step(j, k, row, s_row, u):
                dve.wait_ge(s_row, u)
                if k == 0:
                    dve.tensor_scalar(j, row, ct[:, 0:1], None, ALU.mult).then_inc(s_acc, 1)
                else:
                    dve.scalar_tensor_tensor(out=j, in0=row, scalar=ct[:, k:k + 1], in1=j,
                                             op0=ALU.mult, op1=ALU.add).then_inc(s_acc, 1)

            def rms_diag(n):
                dve.wait_ge(s_sd, n + 1)
                link(dve.reciprocal(rs8[:, n:n + 1], sd8[:, n:n + 1]))
                dve.tensor_scalar(diag[:, n, :], ident, rs8[:, n:n + 1], None, ALU.mult).then_inc(s_diag, 1)

            dve.wait_ge(s_id, 16)
            dve.wait_ge(s_ct, 1)
            for k in range(KT):
                for n in range(2 * k, min(2 * k + 2, NB)):
                    rms_diag(n)
                wait(dve, s_acc, k)
                if k < KT - 1:
                    ada_step(acc[:, 0:2 * D], k, wada1[k][:, :], s_wada1[k], 16)
                else:
                    ada_step(acc[:, D:2 * D], k, wada1[k][:, D:2 * D], s_wada1[k], 16)
                    ada_step(acc[:, 0:D], k, wada1[k][:, 0:D], s_wada1[k + 1], 16)
            def ada_vector(j, bank, turned):
                dst = ada[:, j * KT:(j + 1) * KT]
                dve.wait_ge(s_adat, turned)
                dve.tensor_reduce(dst, ps[:, bank:bank + 2, :].rearrange("p b (m r) -> p (b m) r", r=P), AX_X,
                                  ALU.add).then_inc(s_adar, 1)
                dve.wait_ge(s_adar, turned)
                bias = vec[:, V_BADA + j * KT:V_BADA + (j + 1) * KT]
                if j in (1, 4):
                    gain, a = (V_N1, a1) if j == 1 else (V_N2, a2)
                    link(dve.scalar_tensor_tensor(out=dst, in0=dst, scalar=1.0, in1=bias, op0=ALU.add, op1=ALU.add))
                    link(dve.tensor_tensor(a[:, :], dst, vec[:, gain:gain + KT], ALU.mult))
                else:
                    link(dve.tensor_tensor(dst, dst, bias, ALU.add))

            dve.wait_ge(s_vec, 3)
            ada_vector(1, 2, 1)
            ada_vector(0, 0, 2)

            def low1(u):
                half, k = divmod(u, KT)
                if u % 4 == 3:
                    return
                dve.wait_ge(s_hi1, u + 1)
                dve.tensor_tensor(act_lo[:, k, HALVES[half]], hn[:, k, HALVES[half]],
                                  act_hi[:, k, HALVES[half]].bitcast(F32), ALU.subtract).then_inc(s_act1, 1)

            dve.wait_ge(s_hn, NB)
            for u in range(2 * KT):
                half, k = divmod(u, KT)
                dve.tensor_scalar(hn[:, k, HALVES[half]], hn[:, k, HALVES[half]], a1[:, k:k + 1], ada[:, k:k + 1],
                                  ALU.mult, ALU.add).then_inc(s_v1, 1)
                if u:
                    low1(u - 1)
            low1(2 * KT - 1)

            def qk_norm(tile):
                i = 0 if tile == TK else tile - TQ + 1
                gain = vec[:, V_KG:V_KG + 1] if tile == TK else qg8[:, 0:1]
                for half in range(2):
                    u = 2 * i + half
                    dve.wait_ge(s_sdq, u + 1)
                    wait(dve, s_qn, u - 1)
                    dve.reciprocal(riq[:, half, :], sdq[:, half, :]).then_inc(s_riq, 1)
                    dve.wait_ge(s_riq, u + 1)
                    dve.scalar_tensor_tensor(out=proj[:, tile, HALVES[half]], in0=proj[:, tile, HALVES[half]], scalar=gain,
                                             in1=riq[:, half, :], op0=ALU.mult, op1=ALU.mult).then_inc(s_qn, 1)

            def bias_max(u):
                g, i, lo = u % NKV, u % 2, 0 if u >= NKV else P
                dve.wait_ge(s_sc, u + 1)
                wait(dve, s_pt, u - 1)
                for p in range(GQA):
                    ad = dve.scalar_tensor_tensor(
                        out=pr[i][:, p, lo:], in0=dist[:, lo:], scalar=-SLOPES[g * GQA + p],
                        in1=ps[:, 4 + p // 2, (p % 2) * 256 + lo:(p % 2) * 256 + 256], op0=ALU.mult, op1=ALU.add)
                ad.then_inc(s_add, 1)
                dve.wait_ge(s_add, u + 1)
                link(dve.tensor_reduce(mx[:, i, :], pr[i][:, :, lo:], AX_X, ALU.max))
                heads = slice(g * GQA, (g + 1) * GQA)
                link(dve.scalar_tensor_tensor(out=nm[:, i, :], in0=mx[:, i, :], scalar=-1.0, in1=nsink[:, heads],
                                              op0=ALU.mult, op1=ALU.min))
                dve.tensor_tensor(es[:, i, :], nm[:, i, :], sink[:, heads], ALU.add).then_inc(s_nm, 1)

            def normalise(u):
                i, lo = u % 2, 0 if u >= NKV else P
                dve.wait_ge(s_exp, u + 1)
                link(dve.tensor_tensor(den[:, i, :], den[:, i, :], ex[:, i, :], ALU.add))
                link(dve.reciprocal(rd[:, i, :], den[:, i, :]))
                for p in range(GQA):
                    pn = dve.tensor_scalar(pr[i][:, p, lo:], pr[i][:, p, lo:], rd[:, i, p:p + 1], None, ALU.mult)
                pn.then_inc(s_pn, 1)

            def attn_lo(half):
                for k in range(HK):
                    dve.wait_ge(s_ahi, half * HK + k + 1)
                    dve.tensor_tensor(act_lo[:, k, HALVES[half]], proj[:, TQ + k, HALVES[half]],
                                      act_hi[:, k, HALVES[half]].bitcast(F32), ALU.subtract).then_inc(s_amix, 1)

            def ada_step2(a):
                j, k = divmod(a, KT)
                dve.wait_ge(s_acc, ACC1 + a)
                ada_step(acc[:, j * D:(j + 1) * D], k, wada2[:, a % 2, :], s_wada2[a % 2], 16 * (a // 2 + 1))

            for t in range(N_PROJ):
                u = t - T_ATT
                a = ADA_OPS * (t - 1)
                if 0 <= a < 4 * KT:
                    ada_step2(a)
                if u >= 1:
                    normalise(u - 1)
                if 0 < t < T_ATT:
                    dve.wait_ge(s_wlo, 2)
                    split_next(t)
                if 0 < t <= T_ATT and t - 1 != TV:
                    qk_norm(t - 1)
                if t >= T_ATT:
                    split_next(t)
                if t in ADA_TURN:
                    j = 2 + ADA_TURN[t]
                    ada_vector(j, 6, j + 1)
                if 0 <= a < 4 * KT:
                    ada_step2(a + 1)
                if t == N_PROJ - 1:
                    attn_lo(0)
                    split_next(T_A)
                if u >= 0:
                    bias_max(u)

            def ret_k(n):
                dve.wait_ge(s_rt, n + 1)
                wait(dve, s_kv, n)
                kdec = cst[:, C_KDEC:C_KDEC + RH].unsqueeze(2).broadcast_to([P, RH, P])
                dve.tensor_tensor(kdn[:, :, :], ps[:, 2, :].rearrange("p (h n) -> p h n", h=RH), kdec,
                                  ALU.mult).then_inc(s_kdn, 1)

            def ret_inner(n):
                dve.wait_ge(s_in, n + 1)
                if n:
                    wait(dve, s_o, n)
                if n == 1:
                    dve.wait_ge(s_pt, NU)
                dve.tensor_tensor(flat((inn if n else inn0)[:, :, :]), ps[:, 4, :], cst[:, C_DEC:C_DEC + RH * P],
                                  ALU.mult).then_inc(s_inn, 1)

            def ret_state(n):
                dve.wait_ge(s_kv, n + 1)
                wait(dve, s_o, n)
                new, old = st[(n + 1) % 2], st[n % 2]
                if n == 0:
                    dve.tensor_copy(flat(new[:, :, :]), ps[:, 6, :]).then_inc(s_st, 1)
                    return
                dve.wait_ge(s_st, n)
                for h in range(RH):
                    sn = dve.scalar_tensor_tensor(out=new[:, h, :], in0=old[:, h, :],
                                                  scalar=cst[:, C_CHUNK + h:C_CHUNK + h + 1],
                                                  in1=ps[:, 6, tokens(h)], op0=ALU.mult, op1=ALU.add)
                sn.then_inc(s_st, 1)

            def ret_stats(n):
                dve.wait_ge(s_o, n + 1)
                for h in range(RH):
                    b = dve.bn_stats(bn[:, h, :], ps[:, 5, tokens(h)])
                link(b)
                wait(dve, s_on, n)
                for h in range(RH):
                    b = dve.bn_aggr(mv[:, h, :], bn[:, h, :])
                b.then_inc(s_var, 1)

            def ret_terms(n):
                dve.wait_ge(s_rsd, n + 1)
                dve.wait_ge(s_var, n + 1)
                link(dve.reciprocal(rri[:, :], rsd[:, :]))
                dve.scalar_tensor_tensor(out=nmr[:, :], in0=mv[:, :, 0], scalar=-1.0, in1=rri[:, :],
                                         op0=ALU.mult, op1=ALU.mult).then_inc(s_nmr, 1)

            def ret_gate(n):
                dve.wait_ge(s_ot, n + 1)
                wait(dve, s_rmix, n)
                dve.tensor_tensor(rvl[:, :, :], ps[:, 7, :].rearrange("p (h n) -> p h n", h=RH),
                                  proj[:, RG:RG + RH, tokens(n)], ALU.mult).then_inc(s_rvl, 1)

            def ret_lo(n):
                dve.wait_ge(s_rhi, n + 1)
                dve.tensor_tensor(act_lo[:, HK:, tokens(n)], rvl[:, :, :], act_hi[:, HK:, tokens(n)].bitcast(F32),
                                  ALU.subtract).then_inc(s_rmix, 1)

            def add_a(i):
                m, half = OUT_A[i]
                if half == 0:
                    dve.wait_ge(s_back[m], 16)
                dve.wait_ge(s_mma, i + 1)
                dve.scalar_tensor_tensor(out=x1t[:, m, HALVES[half]], in0=ps[:, i % 2, :],
                                         scalar=ada[:, 2 * KT + m:2 * KT + m + 1], in1=x1t[:, m, HALVES[half]],
                                         op0=ALU.mult, op1=ALU.add).then_inc(s_eva, 1)

            dve.wait_ge(s_evp, N_PROJ)
            ret_k(0)
            ret_inner(0)
            normalise(NU - 1)
            add_a(0)
            add_a(1)
            attn_lo(1)
            for n in range(1, NB + 1):
                if 1 < n < N_OUT - 1 or n == NB:
                    split_next(T_A + n)
                if n >= 2:
                    ret_gate(n - 2)
                if n < NB:
                    ret_state(n - 1)
                ret_stats(n - 1)
                if n < NB:
                    ret_k(n)
                ret_terms(n - 1)
                if n < NB:
                    ret_inner(n)
                if n >= 2:
                    ret_lo(n - 2)
                if n == 1:
                    dve.wait_ge(s_evp, RG + RH)
                    for h in range(RH):
                        dve.tensor_scalar(proj[:, RG + h, :], proj[:, RG + h, :], vec[:, V_RET + h:V_RET + h + 1],
                                          None, ALU.mult).then_inc(s_gate, 1)
                    dve.wait_ge(s_gate, RH)
                    split_next(T_A + n)
                if n < NB:
                    add_a(2 * n)
                if n == N_OUT - 1:
                    split_next(T_A + n)
                if n < NB:
                    add_a(2 * n + 1)

            unit = [0]

            def norm2_lo(u):
                half, k = divmod(u, KT)
                dve.wait_ge(s_hi2, u + 1)
                dve.scalar_tensor_tensor(out=act_lo[:, k, HALVES[half]], in0=ht2[:, u % 2, :],
                                         scalar=ada[:, 3 * KT + k:3 * KT + k + 1],
                                         in1=act_hi[:, k, HALVES[half]].bitcast(F32), op0=ALU.add,
                                         op1=ALU.subtract).then_inc(s_act2, 1)

            def norm2_unit():
                u = unit[0]
                half, k = divmod(u, KT)
                if k == 0:
                    dve.wait_ge(s_sd2, half + 1)
                    link(dve.reciprocal(rinv2[:, half, :], sd2[:, half, :]))
                wait(dve, s_act2, u - 1)
                dve.scalar_tensor_tensor(out=ht2[:, u % 2, :], in0=x1t[:, k, HALVES[half]], scalar=a2[:, k:k + 1],
                                         in1=rinv2[:, half, :], op0=ALU.mult, op1=ALU.mult).then_inc(s_h2, 1)
                if k:
                    norm2_lo(u - 1)
                unit[0] += 1

            for b in range(2 * N_OUT):
                half, m = divmod(b, N_OUT)
                if 1 <= b <= N_OUT:
                    split_next(T_B + b)
                dve.wait_ge(s_mmb, b + 1)
                dve.scalar_tensor_tensor(out=x1t[:, m, HALVES[half]], in0=ps[:, b % 4, :],
                                         scalar=ada[:, 2 * KT + m:2 * KT + m + 1], in1=x1t[:, m, HALVES[half]],
                                         op0=ALU.mult, op1=ALU.add).then_inc(s_evb, 1)
                if b == 2:
                    ret_gate(NB - 1)
                    ret_lo(NB - 1)
                for _ in range(NORM2_UNITS.get(b, 0)):
                    norm2_unit()
            norm2_lo(KT - 1)
            for _ in range(KT):
                norm2_unit()
            norm2_lo(2 * KT - 1)

            def square_split(t, m, q):
                dve.wait_ge(s_evm, t - (T_M - 1))
                wait(dve, s_hid, m + q * KT)
                dve.tensor_tensor(rsq[:, :], rel[:, :], rel[:, :], ALU.mult).then_inc(s_rsq, 1)
                dve.wait_ge(s_hih, m + (q * KT + 1))
                dve.tensor_tensor(tile_of(hid_lo, m), rsq[:, :], tile_of(hid_hi, m).bitcast(F32),
                                  ALU.subtract).then_inc(s_hid, 1)

            def up(q):
                t0 = T_M + q * 2 * KT

                def step(t, slot, count):
                    split_lo(t + 1, 1 - slot)
                    square_split(t, t - t0, q)
                return step

            def down(q):
                t1 = T_M + (q * 2 + 1) * KT

                def step(t, slot, count):
                    if not isinstance(t, int) or t + 1 < N_TILES:
                        split_lo(t + 1, 1 - slot)
                    m = t - t1
                    dve.wait_ge(s_mmm, t - (T_M - 1))
                    if q == QUARTERS - 1:
                        wait(dve, s_ftr, m)
                    dve.scalar_tensor_tensor(out=tile_of(x1t, m) if q < QUARTERS - 1 else fin[:, :], in0=bank_pair(slot),
                                             scalar=ada[:, bass.ds(m + 5 * KT, 1)], in1=tile_of(x1t, m),
                                             op0=ALU.mult, op1=ALU.add).then_inc(s_evm, 1)
                return step

            for q in range(QUARTERS):
                t0 = T_M + q * 2 * KT
                if q == 0:
                    split_lo(t0 + 2, 0)
                    square_split(t0, 0, 0)
                    square_split(t0 + 1, 1, 0)
                    pairs(dve, t0 + 2, KT // 2 - 1, up(0))
                else:
                    pairs(dve, t0, KT // 2, up(q))
                if q < QUARTERS - 1:
                    pairs(dve, t0 + KT, KT // 2, down(q))
            t1 = N_TILES - KT
            for s in range(2):
                down(QUARTERS - 1)(t1 + s, s, 0)
            pairs(dve, t1 + 2, KT // 2 - 2, down(QUARTERS - 1))
            down(QUARTERS - 1)(N_TILES - 2, 0, 0)
            dve.wait_ge(s_ftr, KT - 1)
            for half in range(2):
                dve.wait_ge(s_half, half + 1)
                dve.scalar_tensor_tensor(out=fin[:, HALVES[half]], in0=ps[:, 2 + half, :],
                                         scalar=ada[:, 6 * KT - 1:6 * KT], in1=x1t[:, KT - 1, HALVES[half]],
                                         op0=ALU.mult, op1=ALU.add).then_inc(s_evm, 1)


_INS = ["x", "c", "norm1_g", "norm2_g", "w_ada", "b_ada", "w_in", "q_norm_g", "k_norm_g", "sinks", "ret_norm_g",
        "w_out", "w_mlp1", "w_mlp2"]


def kernel(**inputs):
    import numpy as np
    import concourse.bacc as bacc
    from concourse.bass_utils import run_bass_kernel_spmd as run

    nc = bacc.Bacc("TRN2", target_bir_lowering=False, num_devices=1)
    arrays, args = {}, []
    for name in _INS:
        a = np.ascontiguousarray(inputs[name])
        arrays[f"in_{name}_dram"] = a
        args.append(nc.dram_tensor(f"in_{name}_dram", a.shape, mybir.dt.from_np(a.dtype), kind="ExternalInput").ap())
    arrays["shape_constants"] = shape_constants()
    args.append(nc.dram_tensor("shape_constants", (P, C_W), F32, kind="ExternalInput").ap())
    args.append(nc.dram_tensor("x_spill", (KT, P, S), F32, kind="Internal").ap())
    args.append(nc.dram_tensor("out_0_dram", (1, S, D), F32, kind="ExternalOutput").ap())
    hybrid_layer(nc, *args)
    r = run(nc, [arrays], core_ids=[0])
    return r.results[0]["out_0_dram"]
```
